# Optimizing a Trainium2 kernel written in Bass

```python
import jax, jax.numpy as jnp
from jax import lax
import numpy as np

D_MODEL = 1024
BATCH = 1
SEQ = 512
DEPTH = 1
DEC_BATCH = 8
DEC_SEQ = 1
PAST_LEN = 2048
PAGE_SIZE = 128

HEAD_DIM = 64
MIX_WIDTH = D_MODEL
N_HEADS_A = MIX_WIDTH // (2 * HEAD_DIM)
N_HEADS_B = MIX_WIDTH // (2 * HEAD_DIM)
WIDTH_A = N_HEADS_A * HEAD_DIM
WIDTH_B = N_HEADS_B * HEAD_DIM
DILATED_PATTERNS = ((128, 1), (512, 4), (2048, 16))
WIN_MAX = DILATED_PATTERNS[-1][0]
Q_BLOCK = 128
ROPE_THETA = 10000.0
EPS = 1e-6
SCALE = HEAD_DIM ** -0.5
N_EXPERTS = 64
TOP_K = 8
N_GROUPS = 8
TOPK_GROUPS = 4
D_EXPERT = 256
D_SHARED = 256
ROUTED_SCALE = 2.5
MOE_TOKEN_BLOCK = 512
FORGET_BIAS_LO = 1.0
FORGET_BIAS_HI = 10.0
SPLITS = (WIDTH_A, 2 * WIDTH_A, 3 * WIDTH_A, 3 * WIDTH_A + N_HEADS_A,
          3 * WIDTH_A + N_HEADS_A + WIDTH_B, 3 * WIDTH_A + N_HEADS_A + 2 * WIDTH_B)
IN_COLS = 3 * WIDTH_A + N_HEADS_A + 3 * WIDTH_B
F32 = jnp.float32

kernel_name = 'hymba_fox_dilated_moe_adaln_step'

def _rmsnorm(x, g):
    xf = x.astype(F32)
    y = xf * lax.rsqrt(jnp.mean(xf * xf, axis=-1, keepdims=True) + EPS)
    return (y * g.astype(F32)).astype(x.dtype)

def _softmax_stats(s):
    m = jnp.max(s, axis=-1, keepdims=True)
    e = jnp.exp(s - m)
    l = jnp.sum(e, axis=-1, keepdims=True)
    return e / l, (m + jnp.log(l))[..., 0]

def _rope(x, pos):
    half = HEAD_DIM // 2
    inv = jnp.power(ROPE_THETA, -jnp.arange(half, dtype=F32) * 2.0 / HEAD_DIM)
    ang = pos.astype(F32)[:, None] * inv[None, :]
    cos = jnp.cos(ang)[None, :, None, :]
    sin = jnp.sin(ang)[None, :, None, :]
    xf = x.astype(F32)
    x1, x2 = xf[..., :half], xf[..., half:]
    return jnp.concatenate([x1 * cos - x2 * sin, x2 * cos + x1 * sin], axis=-1).astype(x.dtype)

def _fox_prompt(q, k, v, lf):
    B, S, H, Dh = q.shape
    nb = S // Q_BLOCK
    c = jnp.cumsum(lf, axis=1).transpose(0, 2, 1)
    qb = q.reshape(B, nb, Q_BLOCK, H, Dh).transpose(1, 0, 2, 3, 4)
    cb = c.reshape(B, H, nb, Q_BLOCK).transpose(2, 0, 1, 3)
    kpos = jnp.arange(S)

    def block(args):
        j, qj, cj = args
        s = jnp.einsum('bqhd,bkhd->bhqk', qj, k, preferred_element_type=F32) * SCALE
        s = s + cj[..., :, None] - c[:, :, None, :]
        qpos = j * Q_BLOCK + jnp.arange(Q_BLOCK)
        s = jnp.where(kpos[None, :] <= qpos[:, None], s, -jnp.inf)
        p, _ = _softmax_stats(s)
        return jnp.einsum('bhqk,bkhd->bqhd', p.astype(v.dtype), v)

    o = lax.map(block, (jnp.arange(nb), qb, cb))
    return o.transpose(1, 0, 2, 3, 4).reshape(B, S, H, Dh)

def _fox_decode(q, k_new, v_new, lf_new, cache_k, cache_v, cache_lf, page_table):
    Bd, Sd, H, Dh = q.shape
    n_pages = page_table.shape[1]
    lf_past = cache_lf[page_table].reshape(Bd, n_pages * PAGE_SIZE, H).astype(F32)
    rc = lax.cumsum(lf_past, axis=1, reverse=True)
    r = jnp.concatenate([rc[:, 1:], jnp.zeros((Bd, 1, H), F32)], axis=1)
    dT = jnp.cumsum(lf_new, axis=1).transpose(0, 2, 1)
    s_own = jnp.einsum('bqhd,bkhd->bhqk', q, k_new, preferred_element_type=F32) * SCALE
    s_own = s_own + dT[..., :, None] - dT[..., None, :]
    tri = jnp.arange(Sd)[None, :] <= jnp.arange(Sd)[:, None]
    s_own = jnp.where(tri, s_own, -jnp.inf)
    m0 = jnp.max(s_own, axis=-1)
    p0 = jnp.exp(s_own - m0[..., None])
    l0 = jnp.sum(p0, axis=-1)
    acc0 = jnp.einsum('bhqk,bkhd->bhqd', p0, v_new.astype(F32))
    r_pages = r.reshape(Bd, n_pages, PAGE_SIZE, H).transpose(1, 0, 3, 2)

    def step(carry, xs):
        m, l, acc = carry
        pt, rp = xs
        kp = cache_k[pt]
        vp = cache_v[pt]
        s = jnp.einsum('bqhd,bkhd->bhqk', q, kp, preferred_element_type=F32) * SCALE
        s = s + dT[..., :, None] + rp[:, :, None, :]
        m_new = jnp.maximum(m, jnp.max(s, axis=-1))
        alpha = jnp.exp(m - m_new)
        p = jnp.exp(s - m_new[..., None])
        l = l * alpha + jnp.sum(p, axis=-1)
        acc = acc * alpha[..., None] + jnp.einsum('bhqk,bkhd->bhqd', p, vp.astype(F32))
        return (m_new, l, acc), None

    (m, l, acc), _ = lax.scan(step, (m0, l0, acc0), (page_table.T, r_pages))
    return (acc / l[..., None]).transpose(0, 2, 1, 3).astype(q.dtype)

def _combine_patterns(outs, lses):
    w = jax.nn.softmax(jnp.stack(lses, axis=0), axis=0)
    return jnp.sum(w[..., None] * jnp.stack(outs, axis=0), axis=0)

def _dilated_prompt(q, k, v):
    B, S, H, Dh = q.shape
    outs, lses = [], []
    for window, dil in DILATED_PATTERNS:
        span = window // dil
        blk = span
        unit = dil * blk
        lpad = -(-S // unit) * unit
        m_len = lpad // dil
        nb = m_len // blk

        def strided(t):
            t = jnp.pad(t, ((0, 0), (0, lpad - S), (0, 0), (0, 0)))
            t = t.reshape(B, m_len, dil, H, Dh).transpose(0, 2, 1, 3, 4)
            return t.reshape(B, dil, nb, blk, H, Dh)

        def with_prev(t):
            prev = jnp.pad(t, ((0, 0), (0, 0), (1, 0), (0, 0), (0, 0), (0, 0)))[:, :, :-1]
            return jnp.concatenate([prev, t], axis=3)

        qs = strided(q)
        kk = with_prev(strided(k))
        vv = with_prev(strided(v))
        s = jnp.einsum('brnqhd,brnkhd->brnhqk', qs, kk, preferred_element_type=F32) * SCALE
        qi = jnp.arange(blk)[:, None]
        ki = jnp.arange(2 * blk)[None, :]
        delta = blk + qi - ki
        band = (delta >= 0) & (delta <= span)
        valid = band[None] & ((jnp.arange(nb) > 0)[:, None, None] | (ki >= blk)[None])
        s = jnp.where(valid[None, None, :, None], s, -jnp.inf)
        p, lse = _softmax_stats(s)
        o = jnp.einsum('brnhqk,brnkhd->brnqhd', p.astype(v.dtype), vv, preferred_element_type=F32)
        o = o.reshape(B, dil, m_len, H, Dh).transpose(0, 2, 1, 3, 4).reshape(B, lpad, H, Dh)[:, :S]
        lse = lse.transpose(0, 1, 2, 4, 3).reshape(B, dil, m_len, H).transpose(0, 2, 1, 3).reshape(B, lpad, H)[:, :S]
        outs.append(o)
        lses.append(lse)
    return _combine_patterns(outs, lses).astype(q.dtype)

def _dilated_decode(q, k_new, v_new, buf_k, buf_v):
    Bd, Sd, H, Dh = q.shape
    lb = buf_k.shape[1]
    ek = jnp.concatenate([buf_k, k_new.astype(buf_k.dtype)], axis=1)
    ev = jnp.concatenate([buf_v, v_new.astype(buf_v.dtype)], axis=1)
    outs, lses = [], []
    for window, dil in DILATED_PATTERNS:
        steps = jnp.arange(window // dil + 1) * dil
        idx = lb + jnp.arange(Sd)[:, None] - steps[None, :]
        valid = idx >= 0
        idx = jnp.maximum(idx, 0)
        kg = ek[:, idx]
        vg = ev[:, idx]
        s = jnp.einsum('bqhd,bqkhd->bhqk', q, kg, preferred_element_type=F32) * SCALE
        s = jnp.where(valid[None, None], s, -jnp.inf)
        p, lse = _softmax_stats(s)
        outs.append(jnp.einsum('bhqk,bqkhd->bqhd', p.astype(vg.dtype), vg, preferred_element_type=F32))
        lses.append(lse.transpose(0, 2, 1))
    return _combine_patterns(outs, lses).astype(q.dtype), ek[:, Sd:], ev[:, Sd:]

def _moe(h, w_router, e_bias, w_gate, w_up, w_down, ws_gate, ws_up, ws_down):
    shp = h.shape
    x = h.reshape(-1, shp[-1])
    T = x.shape[0]
    scores = jax.nn.sigmoid((x @ w_router).astype(F32))
    biased = scores + e_bias.astype(F32)
    grouped = biased.reshape(T, N_GROUPS, N_EXPERTS // N_GROUPS)
    group_score = jnp.sum(lax.top_k(grouped, 2)[0], axis=-1)
    _, gsel = lax.top_k(group_score, TOPK_GROUPS)
    gmask = jnp.sum(jax.nn.one_hot(gsel, N_GROUPS, dtype=F32), axis=1) > 0
    emask = jnp.repeat(gmask, N_EXPERTS // N_GROUPS, axis=1)
    _, esel = lax.top_k(jnp.where(emask, biased, -jnp.inf), TOP_K)
    sel = jnp.take_along_axis(scores, esel, axis=1)
    wts = sel / jnp.sum(sel, axis=-1, keepdims=True) * ROUTED_SCALE
    gates = jnp.einsum('tk,tke->te', wts, jax.nn.one_hot(esel, N_EXPERTS, dtype=F32))
    blk = min(MOE_TOKEN_BLOCK, T)
    nb = -(-T // blk)
    tp = nb * blk
    xb = jnp.pad(x, ((0, tp - T), (0, 0))).reshape(nb, blk, shp[-1])
    gb = jnp.pad(gates, ((0, tp - T), (0, 0))).reshape(nb, blk, N_EXPERTS).astype(x.dtype)

    def expert_block(args):
        xt, gt = args
        a = jax.nn.silu(jnp.einsum('td,edf->tef', xt, w_gate)) * jnp.einsum('td,edf->tef', xt, w_up)
        return jnp.einsum('tef,efd->td', a * gt[..., None], w_down)

    routed = lax.map(expert_block, (xb, gb)).reshape(tp, shp[-1])[:T]
    shared = (jax.nn.silu(x @ ws_gate) * (x @ ws_up)) @ ws_down
    return (routed + shared).reshape(shp)

def _run_layer(x, c, pos, attend, w_ada, b_ada, g_norm_mix, g_norm_ffn, w_in, b_f,
               g_qa, g_ka, g_qb, g_kb, g_oa, g_ob, w_o, w_router, e_bias,
               w_gate, w_up, w_down, ws_gate, ws_up, ws_down):
    B, S, _ = x.shape
    mod = jax.nn.silu(c) @ w_ada + b_ada
    sh1, sc1, gt1, sh2, sc2, gt2 = jnp.split(mod[:, None, :], 6, axis=-1)
    h = _rmsnorm(x, g_norm_mix) * (1.0 + sc1) + sh1
    proj = h @ w_in
    qa, ka, va, fa, qb, kb, vb = jnp.split(proj, list(SPLITS), axis=-1)
    qa = _rmsnorm(qa.reshape(B, S, N_HEADS_A, HEAD_DIM), g_qa)
    ka = _rmsnorm(ka.reshape(B, S, N_HEADS_A, HEAD_DIM), g_ka)
    va = va.reshape(B, S, N_HEADS_A, HEAD_DIM)
    lf = jax.nn.log_sigmoid(fa.astype(F32) + b_f.astype(F32))
    qb = _rope(_rmsnorm(qb.reshape(B, S, N_HEADS_B, HEAD_DIM), g_qb), pos)
    kb = _rope(_rmsnorm(kb.reshape(B, S, N_HEADS_B, HEAD_DIM), g_kb), pos)
    vb = vb.reshape(B, S, N_HEADS_B, HEAD_DIM)
    oa, ob, states = attend(qa, ka, va, lf, qb, kb, vb)
    merged = jnp.concatenate([_rmsnorm(oa.reshape(B, S, WIDTH_A), g_oa),
                              _rmsnorm(ob.reshape(B, S, WIDTH_B), g_ob)], axis=-1) @ w_o
    x = x + gt1 * merged
    h2 = _rmsnorm(x, g_norm_ffn) * (1.0 + sc2) + sh2
    x = x + gt2 * _moe(h2, w_router, e_bias, w_gate, w_up, w_down, ws_gate, ws_up, ws_down)
    return x, states

def setup_inputs(seed: int = 0) -> dict:
    key = jax.random.key(seed)
    ks = jax.random.split(key, 32)

    def nrm(i, shape, scale=1.0):
        return scale * jax.random.normal(ks[i], shape, F32)

    n_pages = PAST_LEN // PAGE_SIZE
    n_used = DEC_BATCH * n_pages
    n_phys = n_used + max(1, n_used // 4)
    lb = min(WIN_MAX, PAST_LEN)
    D, E, F, FS = D_MODEL, N_EXPERTS, D_EXPERT, D_SHARED
    forget_bias = jnp.linspace(FORGET_BIAS_LO, FORGET_BIAS_HI, N_HEADS_A, dtype=F32)
    page_table = jax.random.permutation(ks[0], n_phys)[:n_used].reshape(DEC_BATCH, n_pages).astype(jnp.int32)
    return {
        'x_prompt': nrm(1, (BATCH, SEQ, D)),
        'x_sample': nrm(2, (DEC_BATCH, DEC_SEQ, D)),
        'cache_k_a': nrm(3, (DEPTH, n_phys, PAGE_SIZE, N_HEADS_A, HEAD_DIM)),
        'cache_v_a': nrm(4, (DEPTH, n_phys, PAGE_SIZE, N_HEADS_A, HEAD_DIM)),
        'cache_lf_a': jax.nn.log_sigmoid(nrm(5, (DEPTH, n_phys, PAGE_SIZE, N_HEADS_A)) + forget_bias),
        'cache_win_k': nrm(6, (DEPTH, DEC_BATCH, lb, N_HEADS_B, HEAD_DIM)),
        'cache_win_v': nrm(7, (DEPTH, DEC_BATCH, lb, N_HEADS_B, HEAD_DIM)),
        'page_table': page_table,
        'c_prompt': nrm(8, (BATCH, D)),
        'c_sample': nrm(9, (DEC_BATCH, D)),
        'w_ada': nrm(10, (DEPTH, D, 6 * D), 0.5 * D ** -0.5),
        'b_ada': nrm(11, (DEPTH, 6 * D), 0.02),
        'g_norm_mix': 1.0 + nrm(12, (DEPTH, D), 0.02),
        'g_norm_ffn': 1.0 + nrm(13, (DEPTH, D), 0.02),
        'w_in': nrm(14, (DEPTH, D, IN_COLS), D ** -0.5),
        'b_f': forget_bias[None, :] + nrm(15, (DEPTH, N_HEADS_A), 0.1),
        'g_qa': 1.0 + nrm(16, (DEPTH, HEAD_DIM), 0.02),
        'g_ka': 1.0 + nrm(17, (DEPTH, HEAD_DIM), 0.02),
        'g_qb': 1.0 + nrm(18, (DEPTH, HEAD_DIM), 0.02),
        'g_kb': 1.0 + nrm(19, (DEPTH, HEAD_DIM), 0.02),
        'g_oa': 1.0 + nrm(20, (DEPTH, WIDTH_A), 0.02),
        'g_ob': 1.0 + nrm(21, (DEPTH, WIDTH_B), 0.02),
        'w_o': nrm(22, (DEPTH, MIX_WIDTH, D), MIX_WIDTH ** -0.5),
        'w_router': nrm(23, (DEPTH, D, E), D ** -0.5),
        'e_bias': nrm(24, (DEPTH, E), 0.01),
        'w_gate': nrm(25, (DEPTH, E, D, F), D ** -0.5),
        'w_up': nrm(26, (DEPTH, E, D, F), D ** -0.5),
        'w_down': nrm(27, (DEPTH, E, F, D), F ** -0.5),
        'ws_gate': nrm(28, (DEPTH, D, FS), D ** -0.5),
        'ws_up': nrm(29, (DEPTH, D, FS), D ** -0.5),
        'ws_down': nrm(30, (DEPTH, FS, D), FS ** -0.5),
    }

def reference(x_prompt, x_sample, cache_k_a, cache_v_a, cache_lf_a, cache_win_k, cache_win_v,
              page_table, c_prompt, c_sample, w_ada, b_ada, g_norm_mix, g_norm_ffn, w_in, b_f,
              g_qa, g_ka, g_qb, g_kb, g_oa, g_ob, w_o, w_router, e_bias,
              w_gate, w_up, w_down, ws_gate, ws_up, ws_down):
    past_len = page_table.shape[1] * PAGE_SIZE
    pos_p = jnp.arange(x_prompt.shape[1])
    pos_s = past_len + jnp.arange(x_sample.shape[1])
    x_p, x_s = x_prompt, x_sample
    st_p = [[] for _ in range(5)]
    st_s = [[] for _ in range(5)]
    for l in range(DEPTH):
        weights = (w_ada[l], b_ada[l], g_norm_mix[l], g_norm_ffn[l], w_in[l], b_f[l],
                   g_qa[l], g_ka[l], g_qb[l], g_kb[l], g_oa[l], g_ob[l], w_o[l], w_router[l], e_bias[l],
                   w_gate[l], w_up[l], w_down[l], ws_gate[l], ws_up[l], ws_down[l])

        def attend_prompt(qa, ka, va, lf, qb, kb, vb):
            lw = min(WIN_MAX, kb.shape[1])
            oa = _fox_prompt(qa, ka, va, lf)
            ob = _dilated_prompt(qb, kb, vb)
            return oa, ob, (ka, va, lf, kb[:, -lw:], vb[:, -lw:])

        def attend_sample(qa, ka, va, lf, qb, kb, vb, l=l):
            oa = _fox_decode(qa, ka, va, lf, cache_k_a[l], cache_v_a[l], cache_lf_a[l], page_table)
            ob, wk, wv = _dilated_decode(qb, kb, vb, cache_win_k[l], cache_win_v[l])
            return oa, ob, (ka, va, lf, wk, wv)

        x_p, new_p = _run_layer(x_p, c_prompt, pos_p, attend_prompt, *weights)
        x_s, new_s = _run_layer(x_s, c_sample, pos_s, attend_sample, *weights)
        for acc, new in zip(st_p, new_p):
            acc.append(new)
        for acc, new in zip(st_s, new_s):
            acc.append(new)
    k_a_prompt = jnp.stack(st_p[0])
    v_a_prompt = jnp.stack(st_p[1])
    lf_a_prompt = jnp.stack(st_p[2])
    win_k_prompt = jnp.stack(st_p[3])
    win_v_prompt = jnp.stack(st_p[4])
    k_a_sample = jnp.stack(st_s[0])
    v_a_sample = jnp.stack(st_s[1])
    lf_a_sample = jnp.stack(st_s[2])
    win_k_sample = jnp.stack(st_s[3])
    win_v_sample = jnp.stack(st_s[4])
    return (x_p, x_s, k_a_prompt, v_a_prompt, lf_a_prompt, win_k_prompt, win_v_prompt,
            k_a_sample, v_a_sample, lf_a_sample, win_k_sample, win_v_sample)


_drawn_inputs = setup_inputs


def setup_inputs(seed=0):
    import zlib

    import numpy as np

    out = dict(_drawn_inputs(seed))
    spreads = {}
    factors = {'g_norm_mix': 2.882,
     'g_qa': 5.131,
     'g_ka': 2.81,
     'g_qb': 7.07,
     'g_kb': 2.821,
     'g_oa': 18.066,
     'g_ob': 17.679,
     'g_norm_ffn': 3.871}
    for name, (base, spread) in spreads.items():
        noise = np.random.default_rng([zlib.crc32(name.encode()), seed]).standard_normal(out[name].shape)
        drawn = base * np.exp(spread * noise) if base else spread * noise
        out[name] = __import__('jax').numpy.asarray(drawn.astype(out[name].dtype))
    for name, factor in factors.items():
        out[name] = (out[name] * factor).astype(out[name].dtype)
    return out
```

```python
from contextlib import ExitStack

import numpy as np

import concourse.bass as bass
from concourse import mybir
from concourse.alu_op_type import AluOpType as ALU

F32 = mybir.dt.float32
BF16 = mybir.dt.bfloat16
F16 = mybir.dt.float16
I32 = mybir.dt.int32
U32 = mybir.dt.uint32
ACT = mybir.ActivationFunctionType
AX = mybir.AxisListType
ds = bass.ds

P = 128
D = 1024
KC = D // P
SEQ = 512
QB = SEQ // P
NS = 8
T = SEQ + NS
TT = QB + 1
H = 8
DH = 64
W = H * DH
NP = W // P
PAST = 2048
PAGE = 128
PAGES = PAST // PAGE
NPHYS = 160
CH = 4
NCH = PAGES // CH
CKEYS = CH * PAGE
WK = 384
NE = 64
G = 8
F = 256
SLOTS = 128
OVER = -(-T // SLOTS) - 1
EPS = 1e-6
SCALE = DH ** -0.5
BIG = 1e30
ROUTED_SCALE = 2.5
PATTERNS = ((128, 1), (512, 4), (2048, 16))

C_ID, C_HEAD, C_ROT, C_ONE, C_TRI, C_PAGE = (P * n for n in range(6))
C_DIL = 6 * P
C_COS = C_DIL + SEQ
C_SIN = C_COS + SEQ + 1
C_OWNA = C_SIN + SEQ + 1
C_OWNB = C_OWNA + NS * NS
C_PICK = C_OWNB + NS * NS
C_ROW = C_PICK + NP * H
C_DUMP = C_ROW + H
C_LOW = C_DUMP + 1
C_TILES = C_LOW + G * G
C_BF = C_TILES + OVER
N_BF = 3 * P + TT * 3 + 1
NCONST = C_BF + N_BF // 2


def constants():
    c = np.zeros((P, NCONST), np.float32)
    i = np.arange(P)
    c[:, C_ID:C_ID + P] = np.eye(P)
    c[:, C_HEAD:C_HEAD + P] = (i[:, None] // DH == i[None] // DH) / DH
    h = DH // 2
    for m in range(P):
        k = m + h if m % DH < h else m - h
        c[k, C_ROT + m] = -1.0 if m % DH < h else 1.0
    c[:, C_ONE:C_ONE + P] = 1.0
    c[:, C_TRI:C_TRI + P] = np.where(i[None] <= i[:, None], 0.0, -BIG)
    c[:, C_PAGE:C_PAGE + P] = (i[:, None] // PAGES == i[None] // PAGES) & (i[:, None] < i[None])
    back = (SEQ - P) + i[:, None] - np.arange(SEQ)[None]
    seen = sum(((back >= 0) & (back <= w) & (back % d == 0)).astype(np.int64) for w, d in PATTERNS)
    c[:, C_DIL:C_DIL + SEQ] = np.where(seen > 0, np.log(np.maximum(seen, 1)), -BIG)
    inv = np.power(np.float32(10000.0), -np.arange(h, dtype=np.float32) * 2.0 / DH).astype(np.float32)
    pos = np.concatenate([np.arange(SEQ), [PAST]]).astype(np.float32)
    ang = (inv[i % h][:, None] * pos[None]).astype(np.float32)
    c[:, C_COS:C_COS + SEQ + 1] = np.cos(ang.astype(np.float64))
    c[:, C_SIN:C_SIN + SEQ + 1] = np.sin(ang.astype(np.float64))
    own = np.where(np.eye(NS, dtype=bool), 0.0, -BIG).reshape(1, -1)
    c[:, C_OWNA:C_OWNA + NS * NS] = own
    c[:, C_OWNB:C_OWNB + NS * NS] = np.where(own == 0.0, np.log(len(PATTERNS)), own)
    head = 2 * np.arange(NP)[None, :, None] + i[:, None, None] // DH
    c[:, C_PICK:C_PICK + NP * H] = (head == np.arange(H)[None, None]).reshape(P, -1)
    c[:, C_ROW:C_ROW + H] = i[:, None] == np.arange(H)[None]
    c[:, C_DUMP] = T + i
    g = np.arange(G)
    c[:, C_LOW:C_LOW + G * G] = (g[None] < g[:, None]).reshape(-1)
    c[:, C_TILES:C_BF] = SLOTS * np.arange(1, OVER + 1)
    b = np.zeros((P, N_BF), np.float32)
    b[:, :P] = i[:, None] < i[None]
    b[:, P:2 * P] = 1.0
    b[:, 2 * P:3 * P] = i[None]
    tok = np.arange(TT)[None] * P + i[:, None]
    ids = np.stack([tok // 16 * 16, tok % 16, np.ones_like(tok)], -1)
    b[:, 3 * P:N_BF - 1] = ids.reshape(P, -1)
    c[:, C_BF:] = (b.view(np.uint32) >> 16).astype(np.uint16).view(np.float32)
    return c


def program(nc, I, O):
    es = ExitStack()
    with es:
        def sb(name, cols, dt=F32, parts=P):
            return es.enter_context(nc.sbuf_tensor(name, [parts, cols], dt))

        def sem(name):
            return es.enter_context(nc.semaphore(name))

        cst = sb("cst", NCONST)
        cbf = cst[:, C_BF:].bitcast(BF16)
        QKC = 4 * NP
        n_qk, n_v, n_ring = QKC * T, TT * D, 2 * CH * W
        reg_q = sb("reg_q", n_qk + n_v + 2 * n_ring)
        reg_w = sb("reg_w", 3 * KC * 512)
        reg_s = sb("reg_s", 5120)
        X = sb("X", TT * D)
        hTt = sb("hT", KC * T)
        modt = sb("mod", 6 * KC * 9)
        small = sb("small", 984)
        ptab = sb("ptab", P, I32, 1)
        pidx = sb("pidx", 1, U32)
        lfs = sb("lfs", T, F32, H)

        def view(t, at, shape, parts=P):
            n = int(np.prod(shape))
            v = t[0:parts, at:at + n]
            names = "abcd"[:len(shape)]
            if len(shape) > 1:
                v = v.rearrange(f"p ({' '.join(names)}) -> p {' '.join(names)}",
                                **{k: s for k, s in zip(names, shape)})
            return v

        ident = cst[:, C_ID:C_ID + P]
        headmean = cst[:, C_HEAD:C_HEAD + P]
        rotate = cst[:, C_ROT:C_ROT + P]
        ones = cst[:, C_ONE:C_ONE + P]
        tri = cst[:, C_TRI:C_TRI + P]
        laterpg = cst[:, C_PAGE:C_PAGE + P]

        x = view(X, 0, [TT, D])
        hT = view(hTt, 0, [KC, T])
        mod = view(modt, 0, [6 * KC, 9])
        qkT = view(reg_q, 0, [QKC, T])
        v = view(reg_q, n_qk, [TT, D])
        kring = view(reg_q, n_qk + n_v, [2, CH, NP, PAGE])
        vring = view(reg_q, n_qk + n_v + n_ring, [2, CH, W])
        wslot = [view(reg_w, s * KC * 512, [KC, 512]) for s in range(3)]

        def sm(at, shape, parts=P):
            return view(small, at, shape, parts)

        cT = sm(0, [KC, 9])
        cgain = sm(72, [KC, 4])
        gqk = sm(104, [4])
        bada = sm(108, [6 * KC])
        bfc = sm(156, [1], H)
        ss = sm(157, [8])
        rs = sm(165, [8])
        gsc = sm(173, [4])
        sT = sm(177, [KC, 9])
        wf = sm(249, [KC, H])
        ccol = sm(313, [QB, H])
        rl = sm(345, [2, QB])
        nm = sm(353, [2, QB])
        lsum = sm(361, [2, QB])
        dnm = sm(369, [2], H)
        dls = sm(371, [2], H)
        drl = sm(373, [2], H)
        ksel = sm(375, [2, NP, H])
        tot = sm(439, [H])
        otmp = sm(447, [NP, H])
        sqs = sm(480, [KC, NS])
        rsx = sm(544, [2, NS])
        ptot = sm(560, [H])
        ebs = sm(568, [NE])

        pb = [es.enter_context(nc.psum_tensor(f"bank{n}", [P, 512], F32)) for n in range(8)]

        lfr = nc.dram_tensor("suffix_sums", [P, H, PAGE], F32).ap()
        h2d = nc.dram_tensor("h2_rows", [T, D], F32).ap()
        rsum = nc.dram_tensor("routed_sum", [T + SLOTS, D], F32).ap()

        sq = view(reg_s, 0, [2, 512])
        rr = view(reg_s, 1024, [2, 512])
        rope1 = view(reg_s, 2048, [512])
        rope2 = view(reg_s, 2560, [512])
        sqS = sm(632, [QKC, NS])
        rrS = sm(760, [QKC, NS])
        ropeS = sm(888, [2 * NP, NS])
        lfc = view(X, 0, [H, PAGE])
        lfi = view(X, H * PAGE, [H, PAGE])
        knew = view(X, 2048, [W], NS)
        lft = view(reg_s, 0, [5, T], H)
        cum = cst[0:H, C_COS:C_COS + SEQ]
        cumh = cst[0:H, C_SIN:C_SIN + SEQ]
        zero = view(reg_q, n_qk + n_v + n_ring, [64])
        sx = view(reg_s, 0, [2, 512])
        pT = view(reg_s, 1024, [2, QB, P])
        decay = view(reg_s, 2048, [512])
        stage = view(reg_s, 2560, [4, 512])
        sA = view(reg_w, 0, [PAST + NS], H)
        sB = view(reg_w, 2056, [WK + NS], H)
        suffix = view(reg_w, 2456, [PAGES, PAGE], H)
        wink = [view(reg_w, 4504 + 1536 * u, [NP, WK]) for u in range(2)]
        winv = [view(reg_w, 7576 + 1536 * u, [3, W]) for u in range(2)]
        o8 = view(reg_w, 10648, [2, W], H)
        pdA = view(reg_w, 11672, [PAGES, H])
        pdB = view(reg_w, 11800, [3, H])
        pdo = view(reg_w, 11824, [2, H], H)
        RB = view(reg_s, 0, [4, D])
        hst = [view(reg_s, 4096, [D]), view(reg_q, 16384, [D])]
        RS = view(reg_q, 12288, [4, D], NS)
        xres = view(reg_q, 17408, [D])
        diag = view(reg_q, 18432, [2, 4, P])
        junk = view(reg_q, 19456, [D])
        comb = reg_q[:, 20480:20480 + 990].bitcast(BF16).rearrange("p (t e c) -> p t e c", t=TT, c=6)
        wgu = [view(reg_q, 6144 * s, [KC, 2 * F]) for s in range(2)]
        wdn = [view(reg_q, 6144 * s + KC * 2 * F, [2, D]) for s in range(2)]
        wsd = view(reg_w, 0, [2, D])
        wr = view(cst, C_DIL, [KC, NE])
        score = view(reg_w, 2048, [TT, NE])
        bias = view(reg_w, 2368, [TT, NE])
        masked = view(reg_w, 2688, [TT, NE])
        left = view(reg_w, 3008, [TT, NE])
        slot = view(reg_w, 3328, [TT, NE + 2])
        rt = view(reg_w, 3658, [430])
        sg = view(reg_w, 4096, [2, F])
        act2 = view(reg_w, 4096 + 512, [2, F])
        aT = view(reg_w, 4096 + 1024, [2, 2, P])
        xg = view(reg_w, 5632, [2, D])
        xT = view(reg_w, 8192, [2, KC, P])
        y = view(reg_w, 10240, [2, D])

        c_in, small_in, ptab_in, pidx_in = sem("c_in"), sem("small_in"), sem("ptab_in"), sem("pidx_in")
        x_in = sem("x_in")
        group_in = [sem(f"group_in{n}") for n in range(3)]
        group_used = sem("group_used")
        sig_c, silu_c, gains_set, mod_set = sem("sig_c"), sem("silu_c"), sem("gains_set"), sem("mod_set")
        squares, roots, inverses = sem("squares"), sem("roots"), sem("inverses")
        x_scaled, x_turned, hT_set = sem("x_scaled"), sem("x_turned"), sem("hT_set")
        raw_ready, sq_ready, ms_ready, rms_ready = sem("raw_ready"), sem("sq_ready"), sem("ms_ready"), sem("rms_ready")
        rr_set, qk_set, rot_ready, rope_step, rope_set = sem("rr_set"), sem("qk_set"), sem("rot_ready"), sem("rope_step"), sem("rope_set")
        v_ready, v_copied, f_ready = sem("v_ready"), sem("v_copied"), sem("f_ready")
        lf_dve, lf_act, cum_set, cols_turned, cols_set = sem("lf_dve"), sem("lf_act"), sem("cum_set"), sem("cols_turned"), sem("cols_set")
        knew_turned, knew_set = sem("knew_turned"), sem("knew_set")
        lfc_in, lfc_scanned, later_ready, suffix_set, suffix_out = (
            sem("lfc_in"), sem("lfc_scanned"), sem("later_ready"), sem("suffix_set"), sem("suffix_out"))
        win_out, kv_out = sem("win_out"), sem("kv_out")
        zero_set, scattered = sem("zero_set"), sem("scattered")
        ZEROS = 2 * -(-(T + SLOTS) // P)
        k_in = [sem(f"k_in{n}") for n in range(2)]
        v_in = [sem(f"v_in{n}") for n in range(2)]
        wink_in = [sem(f"wink_in{n}") for n in range(2)]
        winv_in = [sem(f"winv_in{n}") for n in range(2)]
        suffix_in = sem("suffix_in")
        q_split, k_scored, w_scored = sem("q_split"), sem("k_scored"), sem("w_scored")
        sA_step, sB_step, sA_max, sB_max = sem("sA_step"), sem("sB_step"), sem("sA_max"), sem("sB_max")
        pA_ready, pB_ready, pA_turned, pB_turned = sem("pA_ready"), sem("pB_ready"), sem("pA_turned"), sem("pB_turned")
        pA_copied, pB_copied, v_used, oB_ready = sem("pA_copied"), sem("pB_copied"), sem("v_used"), sem("oB_ready")
        dl_set, o8_set, o8_turned, o8_step, oT_added = sem("dl_set"), sem("o8_set"), sem("o8_turned"), sem("o8_step"), sem("oT_added")
        staged, cumh_set, decay_ready, decay_set = sem("staged"), sem("cumh_set"), sem("decay_ready"), sem("decay_set")
        s_ready, s_step, s_set, p_ready, p_turned, p_copied = (
            sem("s_ready"), sem("s_step"), sem("s_set"), sem("p_ready"), sem("p_turned"), sem("p_copied"))
        pv_ready, rl_set, heads_set = sem("pv_ready"), sem("rl_set"), sem("heads_set")

        ring = [(12 + n, n % 3) for n in range(6)]
        win_cols = [0, W, 3 * W + H, 4 * W + H, 2 * W, 5 * W + H]

        SQ0, X0, HT0 = TT + 1, TT, KC + 1
        sqs_set, oms_ready, oS_step, oS_set = sem("sqs_set"), sem("oms_ready"), sem("oS_step"), sem("oS_set")
        diag_set, rows_ready, rows_copied = sem("diag_set"), sem("rows_ready"), sem("rows_copied")
        xres_in, proj_ready, proj_read, x1_set = sem("xres_in"), sem("proj_ready"), sem("proj_read"), sem("x1_set")
        h2_step, h2_set = sem("h2_step"), sem("h2_set")
        h2_turned, h2T_set, logit_ready, scored = sem("h2_turned"), sem("h2T_set"), sem("logit_ready"), sem("scored")
        h2_out = [sem(f"h2_out{n}") for n in range(2)]
        wr_in, wsd_in = sem("wr_in"), sem("wsd_in")
        score_clear, route, sel_set, ranked, route_set = sem("score_clear"), sem("route"), sem("sel_set"), sem("ranked"), sem("route_set")
        sgu_ready, ssg_set, sact_set, sa_turned, saT_set, sy_ready, sy_read = (
            sem("sgu_ready"), sem("ssg_set"), sem("sact_set"), sem("sa_turned"), sem("saT_set"), sem("sy_ready"),
            sem("sy_read"))
        wgu_in = [sem(f"wgu_in{n}") for n in range(2)]
        wdn_in = [sem(f"wdn_in{n}") for n in range(2)]
        xg_in = [sem(f"xg_in{n}") for n in range(2)]
        xg_clear, oh_set, id_ready, id_step, gidx_set, sidx_set = (
            sem("xg_clear"), sem("oh_set"), sem("id_ready"), sem("id_step"), sem("gidx_set"), sem("sidx_set"))
        xg_turned, xTa_set, xTb_set, gu_ready, sg_set, act_set = (
            sem("xg_turned"), sem("xTa_set"), sem("xTb_set"), sem("gu_ready"), sem("sg_set"), sem("act_set"))
        a_turned, aT_set, y_ready, yA_set, yB_set, y_free, asked = (
            sem("a_turned"), sem("aT_set"), sem("y_ready"), sem("yA_set"), sem("yB_set"), sem("y_free"), sem("asked"))
        routed_done, r_out = sem("routed_done"), sem("r_out")
        rows_in = [sem(f"rows_in{n}") for n in range(2)]
        y_step, y_set = sem("y_step"), sem("y_set")
        m_over, m_in, m_y = sem("more_known"), sem("more_weights"), sem("more_y")

        idc = [sm(632 + 8 * u, [6]) for u in range(2)]
        ida = sm(648, [4])
        gate = sm(652, [2])
        over_f = sm(654, [2], 1)
        spos = sm(656, [TT])
        gidx = [sb(f"gidx{u}", 1, U32) for u in range(2)]
        sidx = [sb(f"sidx{u}", 1, U32) for u in range(2)]
        over = sb("over", 1, I32, 1)
        m8 = sm(664, [TT * G, 8])
        g8 = view(rt, 0, [TT, G])
        grank = view(rt, 40, [TT, G])
        top8 = view(rt, 80, [TT, 8])
        gsum = view(rt, 120, [TT])
        cnt = view(rt, 128, [NE], 1)
        pair = left.rearrange("p t (a b) -> p t a b", a=G)
        pair2 = view(reg_q, 19456, [TT, G, G])
        rem = view(reg_q, 19456, [TT, NE])
        oh = reg_q[:, 18432:18432 + TT * SLOTS // 2].bitcast(BF16).rearrange("p (t s) -> p t s", t=TT)
        selb = reg_q[:, 19000:19000 + TT * NE // 2].bitcast(BF16).rearrange("p (t e) -> p t e", t=TT)
        before = cbf[:, 0:P]
        onesb = cbf[:, P:2 * P]
        slotno = cbf[:, 2 * P:3 * P]
        tokid = cbf[:, 3 * P:N_BF - 1].rearrange("p (t c) -> p t c", c=3)
        gidx1 = [g[:, 0:1] for g in gidx]
        sidx1 = [g[:, 0:1] for g in sidx]
        rows_of = [P] * QB + [NS]
        ROWS = ((0, 2), (1, 4), (2, 3), (3, 5))

        def row(v_, t, c0, n):
            return RB[:, v_, c0:c0 + n] if t < QB else RS[:, v_, c0:c0 + n]

        def tensor_after(pe):
            mm, turn = nc.tensor.matmul, nc.tensor.transpose
            pe.wait_ge(o8_set, 2 + 2 * NS)
            for j in range(8):
                pe.wait_ge(diag_set, j + 1)
                if j >= 2:
                    pe.wait_ge(rows_copied, j - 1)
                mm(pb[j % 2][:, :], lhsT=ones, rhs=diag[:, j % 2, :, :].rearrange("p a b -> p (a b)"), start=True, stop=True
                   ).then_inc(rows_ready, 1)
            pe.wait_ge(pB_copied, 1 + NS)
            pe.wait_ge(s_set, 2 + 2 * QB * NS)
            for j in range(8):
                if j >= 2:
                    pe.wait_ge(rows_copied, 8 + j - 1)
                for c in range(4):
                    last = turn(pb[2 + j % 2][0:NS, c * P:c * P + P], mod[:, ROWS[j // 2][1] * KC + j % 2 * 4 + c, 1:9], ident)
                last.then_inc(rows_ready, 1)
            pe.wait_ge(oT_added, 1 + NS)
            pe.wait_ge(x_scaled, X0 + 2 * QB)
            for c in range(KC):
                if c >= 2:
                    pe.wait_ge(hT_set, HT0 + c - 1)
                for t in range(QB):
                    last = turn(pb[4 + c % 2][:, t * P:t * P + P], x[:, t, c * P:c * P + P], ident)
                last.then_inc(x_turned, 1)
            pe.wait_ge(p_copied, 1 + 2 * QB * NS)
            pe.wait_ge(sqs_set, 1)
            for m in range(2):
                for c in range(NP):
                    last = mm(pb[6][:, m * NS:m * NS + NS], lhsT=ones, rhs=sqs[:, m * NP + c, :], start=(c == 0), stop=(c == NP - 1))
            last.then_inc(oms_ready, 1)

            def project(t):
                n_ = rows_of[t]
                if t == QB:
                    pe.wait_ge(oS_set, 1)
                for h in range(2):
                    n = 2 * t + h
                    if t == 0:
                        pe.wait_ge(group_in[h], 16 * 7)
                    if n >= 4:
                        pe.wait_ge(proj_read, n - 3)
                    for k in range(KC):
                        last = mm(pb[n % 4][0:n_, :], lhsT=hT[:, k, t * P:t * P + n_], rhs=wslot[h][:, k, :],
                                  start=(k == 0), stop=(k == KC - 1))
                    last.then_inc(proj_ready, 1)

            def turn_h2(t):
                n_ = rows_of[t]
                pe.wait_ge(h2_set, t + 1)
                for hh in range(2):
                    if t >= 1:
                        pe.wait_ge(h2T_set, 2 * t - 1 + hh)
                    for c in range(4):
                        last = turn(pb[4 + hh][:, c * P:c * P + n_], hst[t % 2][0:n_, (hh * 4 + c) * P:(hh * 4 + c + 1) * P],
                                    ident[0:n_, 0:n_])
                    last.then_inc(h2_turned, 1)

            def logits(t):
                n_ = rows_of[t]
                pe.wait_ge(h2T_set, 2 * t + 2)
                if t == 0:
                    pe.wait_ge(wr_in, 16)
                    pe.wait_ge(roots, 3)
                for k in range(KC):
                    last = mm(pb[6][0:n_, t * NE:t * NE + NE], lhsT=hT[:, k, t * P:t * P + n_], rhs=wr[:, k, :],
                              start=(k == 0), stop=(k == KC - 1))
                last.then_inc(logit_ready, 1)

            pe.wait_ge(rows_copied, 16)
            pe.wait_ge(hT_set, HT0 + KC)
            for t in range(TT + 2):
                if t < TT:
                    project(t)
                if 1 <= t <= TT:
                    turn_h2(t - 1)
                if t >= 2:
                    logits(t - 2)

            def shared_gu(t):
                n_ = rows_of[t]
                if t == 0:
                    pe.wait_ge(proj_read, 2 * TT)
                    pe.wait_ge(group_in[2], 16 * 7)
                if t >= 2:
                    pe.wait_ge(sact_set, t - 1)
                for k in range(KC):
                    last = mm(pb[t % 2][0:n_, :], lhsT=hT[:, k, t * P:t * P + n_], rhs=wslot[2][:, k, :],
                              start=(k == 0), stop=(k == KC - 1))
                last.then_inc(sgu_ready, 1)

            def shared_down(t):
                n_ = rows_of[t]
                pe.wait_ge(sact_set, t + 1)
                if t >= 1:
                    pe.wait_ge(saT_set, t)
                for c in range(2):
                    last = turn(pb[2][:, c * P:c * P + n_], act2[0:n_, t % 2, c * P:c * P + P], ident[0:n_, 0:n_])
                last.then_inc(sa_turned, 1)
                if t == 0:
                    rank()
                pe.wait_ge(saT_set, t + 1)
                if t == 0:
                    pe.wait_ge(wsd_in, 16)
                for hh in range(2):
                    if t >= 1:
                        pe.wait_ge(sy_read, 2 * t - 1 + hh)
                    for c in range(2):
                        last = mm(pb[4 + hh][0:n_, :], lhsT=aT[:, t % 2, c, 0:n_], rhs=wsd[:, c, hh * 512:hh * 512 + 512],
                                  start=(c == 0), stop=(c == 1))
                    last.then_inc(sy_ready, 1)

            def rank():
                pe.wait_ge(sel_set, 1)
                for t in range(TT):
                    n_ = rows_of[t]
                    for t2 in range(t):
                        mm(pb[3][0:n_, t * NE:t * NE + NE], lhsT=onesb[:, 0:n_], rhs=selb[:, t2, :], start=(t2 == 0), stop=False)
                    mm(pb[3][0:n_, t * NE:t * NE + NE], lhsT=before[0:n_, 0:n_], rhs=selb[0:n_, t, :], start=(t == 0), stop=True)
                for t in range(TT):
                    last = mm(pb[3][0:1, TT * NE:(TT + 1) * NE], lhsT=onesb[0:rows_of[t], 0:1], rhs=selb[0:rows_of[t], t, :],
                              start=(t == 0), stop=(t == QB))
                last.then_inc(ranked, 1)

            shared_gu(0)
            shared_gu(1)
            for t in range(TT):
                shared_down(t)
                if t + 2 < TT:
                    shared_gu(t + 2)

            for e in range(2):
                pe.wait_ge(oh_set, e + 1)
                if e == 0:
                    pe.wait_ge(sy_read, 2 * TT)
                else:
                    pe.wait_ge(id_step, 1)
                for t in range(TT):
                    n_ = rows_of[t]
                    last = mm(pb[5][:, 0:6], lhsT=oh[0:n_, t, :], rhs=comb[0:n_, t, e, :], start=(t == 0), stop=(t == QB))
                last.then_inc(id_ready, 1)
            pe.wait_ge(xg_in[0], 16)
            pe.wait_ge(saT_set, TT)
            pe.wait_ge(route_set, 2)
            for hh in range(2):
                for c in range(4):
                    last = turn(pb[2 + hh][:, c * P:c * P + P], xg[:, 0, (hh * 4 + c) * P:(hh * 4 + c + 1) * P], ident)
                last.then_inc(xg_turned, 1)
            pe.sem_inc(y_ready, 2)
            with pe.Fori(0, NE // 2) as i:
                for u in range(2):
                    e = i * 2 + u
                    pe.wait_ge(wgu_in[u], i * 16 + 16)
                    pe.wait_ge(xTa_set, i * 2 + (u + 1))
                    pe.wait_ge(xTb_set, i * 2 + (u + 1))
                    pe.wait_ge(act_set, i * 2 + (u + 1))
                    for k in range(KC):
                        last = mm(pb[u][:, :], lhsT=xT[:, u, k, :], rhs=wgu[u][:, k, :], start=(k == 0), stop=(k == KC - 1))
                    last.then_inc(gu_ready, 1)
                    pe.wait_ge(xg_in[1 - u], i * 16 + 16 * (u + 1))
                    for hh in range(2):
                        for c in range(4):
                            last = turn(pb[2 + hh][:, c * P:c * P + P], xg[:, 1 - u, (hh * 4 + c) * P:(hh * 4 + c + 1) * P], ident)
                        last.then_inc(xg_turned, 1)
                    pe.wait_ge(act_set, i * 2 + (u + 3))
                    pe.wait_ge(aT_set, i * 2 + (u + 1))
                    for c in range(2):
                        last = turn(pb[4][:, c * P:c * P + P], act2[:, u, c * P:c * P + P], ident)
                    last.then_inc(a_turned, 1)
                    pe.wait_ge(oh_set, i * 2 + (u + 3))
                    pe.wait_ge(id_step, i * 2 + (u + 2))
                    for t in range(TT):
                        n_ = rows_of[t]
                        last = mm(pb[5][:, 0:6], lhsT=oh[0:n_, t, :],
                                  rhs=comb[0:n_, t, ds(i * 2 + (u + 2), 1), :].rearrange("p a b -> p (a b)"),
                                  start=(t == 0), stop=(t == QB))
                    last.then_inc(id_ready, 1)
                    pe.wait_ge(aT_set, i * 2 + (u + 2))
                    pe.wait_ge(wdn_in[u], i * 16 + 16)
                    for hh in range(2):
                        pe.wait_ge(yB_set if hh else yA_set, i * 2 + (u + 1))
                        for c in range(2):
                            last = mm(pb[6 + hh][:, :], lhsT=aT[:, u, c, :], rhs=wdn[u][:, c, hh * 512:hh * 512 + 512],
                                      start=(c == 0), stop=(c == 1))
                        last.then_inc(y_ready, 1)

            pe.wait_ge(m_over, 1)
            pe.wait_ge(yB_set, NE + 1)
            pe.wait_ge(yA_set, NE + 1)
            pe.wait_ge(aT_set, NE + 1)
            pe.wait_ge(id_step, NE + 2)
            more = pe.value_load(over[0:1, 0:1], min_val=0, max_val=OVER)
            with pe.If(more > 0):
                with pe.Fori(0, more) as i:
                    with pe.Fori(0, NE) as e:
                        j = i * NE + e
                        pe.wait_ge(oh_set, j + (NE + 2 + 1))
                        for t in range(TT):
                            n_ = rows_of[t]
                            last = mm(pb[5][:, 0:6], lhsT=oh[0:n_, t, :],
                                      rhs=comb[0:n_, t, ds(e, 1), :].rearrange("p a b -> p (a b)"), start=(t == 0), stop=(t == QB))
                        last.then_inc(id_ready, 1)
                        pe.wait_ge(xg_in[0], j * 16 + (16 * (NE // 2 + 1) + 16))
                        for hh in range(2):
                            for c in range(4):
                                last = turn(pb[2 + hh][:, c * P:c * P + P], xg[:, 0, (hh * 4 + c) * P:(hh * 4 + c + 1) * P], ident)
                        last.then_inc(xg_turned, 1)
                        pe.wait_ge(xTa_set, j + (NE + 1 + 1))
                        pe.wait_ge(m_in, j * 32 + 32)
                        for k in range(KC):
                            last = mm(pb[0][:, :], lhsT=xT[:, 0, k, :], rhs=wgu[0][:, k, :], start=(k == 0), stop=(k == KC - 1))
                        last.then_inc(gu_ready, 1)
                        pe.wait_ge(act_set, j + (NE + 2 + 1))
                        for c in range(2):
                            last = turn(pb[4][:, c * P:c * P + P], act2[:, 0, c * P:c * P + P], ident)
                        last.then_inc(a_turned, 1)
                        pe.wait_ge(aT_set, j + (NE + 1 + 1))
                        for hh in range(2):
                            for c in range(2):
                                last = mm(pb[6 + hh][:, :], lhsT=aT[:, 0, c, :], rhs=wdn[0][:, c, hh * 512:hh * 512 + 512],
                                          start=(c == 0), stop=(c == 1))
                        last.then_inc(y_ready, 1)

        def vector_after(dve):
            V = nc.vector
            for j in range(8):
                if j >= 2:
                    dve.wait_ge(rows_ready, j - 1)
                k = ROWS[j // 2][1] * KC + j % 2 * 4
                V.tensor_tensor(diag[:, j % 2, :, :], ident.unsqueeze(1).broadcast_to([P, 4, P]),
                                mod[:, k:k + 4, 0:1].broadcast_to([P, 4, P]), ALU.mult).then_inc(diag_set, 1)
            dve.wait_ge(roots, 2)
            V.reciprocal(rs[:, :], ss[:, :]).then_inc(inverses, 1)
            dve.wait_ge(inverses, 3)
            for n in range(2 * QB):
                t, m = n // 2, n % 2
                V.tensor_scalar(x[:, t, m * W:m * W + W], x[:, t, m * W:m * W + W], rs[:, n:n + 1], None, ALU.mult
                                ).then_inc(x_scaled, 1)
            oS = hT[:, :, SEQ:T]
            V.tensor_tensor(sqs, oS, oS, ALU.mult).then_inc(sqs_set, 1)
            dve.wait_ge(roots, 3)
            V.reciprocal(rsx, rsx).then_inc(oS_step, 1)
            dve.wait_ge(oS_step, 1)
            for m in range(2):
                V.tensor_tensor(oS[:, m * NP:m * NP + NP, :], oS[:, m * NP:m * NP + NP, :],
                                rsx[:, m:m + 1, :].broadcast_to([P, NP, NS]), ALU.mult).then_inc(oS_step, 1)
            dve.wait_ge(oS_step, 3)
            V.tensor_tensor(oS, oS, cgain[:, :, 2:3].broadcast_to([P, KC, NS]), ALU.mult).then_inc(oS_set, 1)
            V.memset(comb[:, :, NE:, :], 0.0).then_inc(route, 1)
            for t in range(TT):
                V.tensor_copy(comb[:, t, 0:NE, 0:3], tokid[:, t:t + 1, :].broadcast_to([P, NE, 3])).then_inc(route, 1)
            dve.wait_ge(rows_copied, 16)

            def residual(t):
                n_ = rows_of[t]
                for h in range(2):
                    n = 2 * t + h
                    xo = x[0:n_, t, h * 512:h * 512 + 512]
                    dve.wait_ge(proj_ready, n + 1)
                    V.tensor_tensor(xo, pb[n % 4][0:n_, :], row(0, t, h * 512, 512), ALU.mult).then_inc(proj_read, 1)
                    dve.wait_ge(proj_read, n + 1)
                    dve.wait_ge(xres_in, 16 * (t + 1))
                    V.tensor_tensor(xo, xo, xres[0:n_, h * 512:h * 512 + 512], ALU.add).then_inc(x1_set, 1)

            def norm2(t):
                n_ = rows_of[t]
                dve.wait_ge(roots, t + 4)
                V.reciprocal(rs[0:n_, t:t + 1], ss[0:n_, t:t + 1]).then_inc(inverses, 1)
                dve.wait_ge(inverses, t + 4)
                if t >= 2:
                    dve.wait_ge(h2_out[t % 2], 16 * (t // 2))
                    dve.wait_ge(h2_turned, 2 * t - 2)
                hd = hst[t % 2][0:n_, :]
                V.scalar_tensor_tensor(out=hd, in0=x[0:n_, t, :], scalar=rs[0:n_, t:t + 1], in1=row(1, t, 0, D),
                                       op0=ALU.mult, op1=ALU.mult).then_inc(h2_step, 1)
                dve.wait_ge(h2_step, t + 1)
                V.tensor_tensor(hd, hd, row(2, t, 0, D), ALU.add).then_inc(h2_set, 1)

            for t in range(TT + 1):
                if t < TT:
                    residual(t)
                if t >= 1:
                    norm2(t - 1)

            V.memset(score, 0.5).then_inc(score_clear, 1)
            V.memset(slot, -1.0).then_inc(route, 1)
            r = 7
            dve.wait_ge(scored, 2)
            dve.wait_ge(route, r)
            V.tensor_tensor(bias, score, ebs.unsqueeze(1).broadcast_to([P, TT, NE]), ALU.add).then_inc(route, 1)
            dve.wait_ge(route, r + 1)
            for t in range(TT):
                for g in range(G):
                    V.max(m8[:, t * G + g, :], bias[:, t, g * 8:g * 8 + 8]).then_inc(route, 1)
            r += 1 + TT * G
            dve.wait_ge(route, r)
            V.tensor_tensor(g8.rearrange("p a b -> p (a b)"), m8[:, :, 0], m8[:, :, 1], ALU.add).then_inc(route, 1)
            dve.wait_ge(route, r + 1)
            for t in range(TT):
                V.tensor_tensor(pair[:, t, :, :], g8[:, t:t + 1, :].broadcast_to([P, G, G]),
                                g8[:, t, :].unsqueeze(2).broadcast_to([P, G, G]), ALU.is_gt).then_inc(route, 1)
                V.tensor_tensor(pair2[:, t, :, :], g8[:, t:t + 1, :].broadcast_to([P, G, G]),
                                g8[:, t, :].unsqueeze(2).broadcast_to([P, G, G]), ALU.is_equal).then_inc(route, 1)
            r += 1 + 2 * TT
            dve.wait_ge(route, r)
            low = cst[:, C_LOW:C_LOW + G * G]
            V.tensor_tensor(pair2.rearrange("p t a b -> p t (a b)"), pair2.rearrange("p t a b -> p t (a b)"),
                            low.unsqueeze(1).broadcast_to([P, TT, G * G]), ALU.mult).then_inc(route, 1)
            dve.wait_ge(route, r + 1)
            V.tensor_tensor(left, left, pair2.rearrange("p t a b -> p t (a b)"), ALU.add).then_inc(route, 1)
            dve.wait_ge(route, r + 2)
            V.reduce_sum(grank.rearrange("p a b -> p (a b)"), pair.rearrange("p t a b -> p (t a) b"), AX.X).then_inc(route, 1)
            dve.wait_ge(route, r + 3)
            V.tensor_scalar(grank, grank, 3.5, BIG, ALU.is_lt, ALU.mult).then_inc(route, 1)
            dve.wait_ge(route, r + 4)
            V.tensor_scalar(grank, grank, -BIG, None, ALU.add).then_inc(route, 1)
            dve.wait_ge(route, r + 5)
            for t in range(TT):
                V.tensor_tensor(masked[:, t, :].rearrange("p (a b) -> p a b", a=G), bias[:, t, :].rearrange("p (a b) -> p a b", a=G),
                                grank[:, t, :].unsqueeze(2).broadcast_to([P, G, 8]), ALU.add).then_inc(route, 1)
            r += 5 + TT
            dve.wait_ge(route, r)
            for t in range(TT):
                V.max(top8[:, t, :], masked[:, t, :]).then_inc(route, 1)
            r += TT
            dve.wait_ge(route, r)
            for t in range(TT):
                V.match_replace(left[:, t, :], top8[:, t, :], masked[:, t, :], -2 * BIG).then_inc(route, 1)
            r += TT
            dve.wait_ge(route, r)
            V.tensor_tensor(left, left, masked, ALU.not_equal).then_inc(route, 1)
            dve.wait_ge(route, r + 1)
            V.tensor_copy(selb, left).then_inc(sel_set, 1)
            V.tensor_tensor(score, score, left, ALU.mult).then_inc(route, 1)
            dve.wait_ge(route, r + 2)
            V.reduce_sum(gsum, score, AX.X).then_inc(route, 1)
            dve.wait_ge(route, r + 3)
            V.reciprocal(gsum, gsum).then_inc(route, 1)
            dve.wait_ge(route, r + 4)
            V.scalar_tensor_tensor(out=score, in0=score, scalar=ROUTED_SCALE, in1=gsum.unsqueeze(2).broadcast_to([P, TT, NE]),
                                   op0=ALU.mult, op1=ALU.mult).then_inc(route, 1)
            r += 5
            src = score
            for n in range(3):
                dve.wait_ge(route, r)
                V.tensor_copy(comb[:, :, 0:NE, 3 + n], src).then_inc(route, 1)
                r += 1
                if n < 2:
                    dve.wait_ge(route, r)
                    V.tensor_tensor(rem, src, comb[:, :, 0:NE, 3 + n], ALU.subtract).then_inc(route, 1)
                    r += 1
                    src = rem

            def shared_act(t):
                n_ = rows_of[t]
                dve.wait_ge(ssg_set, t + 1)
                V.tensor_tensor(act2[0:n_, t % 2, :], pb[t % 2][0:n_, F:2 * F], sg[0:n_, t % 2, :], ALU.mult).then_inc(sact_set, 1)

            def shared_add(t):
                n_ = rows_of[t]
                for hh in range(2):
                    n = 2 * t + hh
                    dve.wait_ge(sy_ready, n + 1)
                    if n >= 1:
                        dve.wait_ge(x1_set, 2 * TT + n)
                    else:
                        dve.wait_ge(route, r)
                    V.tensor_tensor(junk[0:n_, 0:512], pb[4 + hh][0:n_, :], row(3, t, hh * 512, 512), ALU.mult).then_inc(sy_read, 1)
                    dve.wait_ge(sy_read, n + 1)
                    xo = x[0:n_, t, hh * 512:hh * 512 + 512]
                    V.tensor_tensor(xo, xo, junk[0:n_, 0:512], ALU.add).then_inc(x1_set, 1)

            shared_act(0)
            shared_act(1)
            dve.wait_ge(ranked, 1)
            V.scalar_tensor_tensor(out=slot[:, 0:QB, 0:NE], in0=pb[3][:, 0:QB * NE].rearrange("p (a b) -> p a b", b=NE),
                                   scalar=1.0, in1=left[:, 0:QB, :], op0=ALU.add, op1=ALU.mult).then_inc(route, 1)
            V.scalar_tensor_tensor(out=slot[0:NS, QB, 0:NE], in0=pb[3][0:NS, QB * NE:TT * NE],
                                   scalar=1.0, in1=left[0:NS, QB, :], op0=ALU.add, op1=ALU.mult).then_inc(route, 1)
            V.reduce_max(over_f[:, 0:1], pb[3][0:1, TT * NE:(TT + 1) * NE], AX.X).then_inc(route_set, 1)
            dve.wait_ge(route, r + 2)
            dve.wait_ge(route_set, 1)
            V.tensor_scalar(slot[:, 0:QB, 0:NE], slot[:, 0:QB, 0:NE], -1.0, None, ALU.add).then_inc(route, 1)
            V.tensor_scalar(slot[0:NS, QB, 0:NE], slot[0:NS, QB, 0:NE], -1.0, None, ALU.add).then_inc(route, 1)
            V.tensor_scalar(cnt[:, 0:OVER], cst[0:1, C_TILES:C_TILES + OVER], over_f[:, 0:1], None, ALU.is_lt).then_inc(route, 1)
            r += 5
            dve.wait_ge(route, r)
            V.reduce_sum(over_f[:, 1:2], cnt[:, 0:OVER], AX.X).then_inc(route, 1)
            dve.wait_ge(route, r + 1)
            V.tensor_copy(over[0:1, 0:1], over_f[:, 1:2]).then_inc(route_set, 1)
            V.memset(xg.rearrange("p a b -> p (a b)"), 0.0).then_inc(xg_clear, 1)

            def onehot(e):
                for t in range(TT):
                    n_ = rows_of[t]
                    last = V.tensor_scalar(oh[0:n_, t, :], slotno[0:n_, :], slot[0:n_, t, ds(e, 1)], None, ALU.is_equal)
                    if t < QB:
                        last.then_inc(route, 1)
                last.then_inc(oh_set, 1)

            def place_ids(u, done, base, signal, where, gout):
                V.reduce_sum(ida[:, 0:1], idc[u][:, 0:2], AX.X).then_inc(done, 1)
                V.tensor_scalar(ida[:, 1:2], idc[u][:, 2:3], -1.0, 1.0, ALU.mult, ALU.add).then_inc(done, 1)
                V.reduce_sum(gout, idc[u][:, 3:6], AX.X).then_inc(done, 1)
                dve.wait_ge(done, base)
                V.scalar_tensor_tensor(out=where, in0=ida[:, 1:2], scalar=cst[:, C_DUMP:C_DUMP + 1], in1=ida[:, 0:1],
                                       op0=ALU.mult, op1=ALU.add).then_inc(signal, 1)

            for e in range(2):
                if e:
                    dve.wait_ge(id_ready, e)
                onehot(e)
                if e == 0:
                    for t in range(TT):
                        shared_add(t)
                        if t + 2 < TT:
                            shared_act(t + 2)
                dve.wait_ge(id_ready, e + 1)
                V.tensor_copy(idc[e], pb[5][:, 0:6]).then_inc(id_step, 1)
                dve.wait_ge(id_step, e + 1)
                place_ids(e, sidx_set, 3 * e + 3, gidx_set, gidx1[e], gate[:, e:e + 1])
            dve.sem_inc(act_set, 2)
            dve.sem_inc(yB_set, 1)
            dve.wait_ge(xg_turned, 2)
            V.tensor_copy(xT[:, 0, 4:8, :].rearrange("p a b -> p (a b)"), pb[3][:, :]).then_inc(xTb_set, 1)
            with dve.Fori(0, NE // 2) as i:
                for u in range(2):
                    dve.wait_ge(id_ready, i * 2 + (u + 2))
                    onehot(i * 2 + (u + 2))
                    dve.wait_ge(sg_set, i * 2 + (u + 1))
                    dve.wait_ge(gidx_set, i * 2 + (u + 1))
                    V.scalar_tensor_tensor(out=act2[:, u, :], in0=pb[u][:, F:2 * F], scalar=gate[:, u:u + 1], in1=sg[:, u, :],
                                           op0=ALU.mult, op1=ALU.mult).then_inc(act_set, 1)
                    dve.wait_ge(xg_turned, i * 4 + (2 * u + 4))
                    V.tensor_copy(xT[:, 1 - u, 4:8, :].rearrange("p a b -> p (a b)"), pb[3][:, :]).then_inc(xTb_set, 1)
                    dve.wait_ge(y_free, i * 2 + (u + 1))
                    V.tensor_copy(sidx1[u], gidx1[u]).then_inc(sidx_set, 1)
                    dve.wait_ge(id_ready, i * 2 + (u + 3))
                    V.tensor_copy(idc[u], pb[5][:, 0:6]).then_inc(id_step, 1)
                    dve.wait_ge(id_step, i * 2 + (u + 3))
                    dve.wait_ge(act_set, i * 2 + (u + 3))
                    dve.wait_ge(sidx_set, i * 8 + (4 * u + 7))
                    dve.wait_ge(xg_in[u], i * 16 + 16)
                    place_ids(u, sidx_set, i * 8 + (4 * u + 10), gidx_set, gidx1[u], gate[:, u:u + 1])
                    dve.wait_ge(y_ready, i * 4 + (2 * u + 4))
                    V.tensor_copy(y[:, u, 512:1024], pb[7][:, :]).then_inc(yB_set, 1)

            dve.wait_ge(xg_turned, 2 * NE + 2)
            dve.wait_ge(id_ready, NE + 2)
            dve.wait_ge(y_ready, 2 * NE + 2)
            dve.wait_ge(scattered, 16 * (ZEROS + NE))
            dve.sem_inc(m_over, 1)
            more = dve.value_load(over[0:1, 0:1], min_val=0, max_val=OVER)
            with dve.If(more > 0):
                with dve.Fori(0, more) as i:
                    V.tensor_scalar(slot, slot, -float(SLOTS), None, ALU.add).then_inc(m_y, 1)
                    with dve.Fori(0, NE) as e:
                        j = i * NE + e
                        dve.wait_ge(scattered, j * 16 + 16 * (ZEROS + NE))
                        dve.wait_ge(m_y, i * (NE + 1) + 1)
                        for t in range(TT):
                            n_ = rows_of[t]
                            last = V.tensor_scalar(oh[0:n_, t, :], slotno[0:n_, :], slot[0:n_, t, ds(e, 1)], None, ALU.is_equal)
                            if t < QB:
                                last.then_inc(route, 1)
                        last.then_inc(oh_set, 1)
                        dve.wait_ge(id_ready, j + (NE + 2 + 1))
                        V.tensor_copy(idc[0], pb[5][:, 0:6]).then_inc(id_step, 1)
                        dve.wait_ge(id_step, j + (NE + 3))
                        place_ids(0, sidx_set, j * 3 + (4 * NE + 6 + 3), gidx_set, gidx1[0], gate[:, 0:1])
                        dve.wait_ge(xg_turned, j + (2 * NE + 2 + 1))
                        V.tensor_copy(xT[:, 0, 4:8, :].rearrange("p a b -> p (a b)"), pb[3][:, :]).then_inc(xTb_set, 1)
                        dve.wait_ge(xTb_set, j + (NE + 2))
                        V.tensor_copy(xT[:, 0, 0:4, :].rearrange("p a b -> p (a b)"), pb[2][:, :]).then_inc(xTa_set, 1)
                        dve.wait_ge(sg_set, j + (NE + 1))
                        V.scalar_tensor_tensor(out=act2[:, 0, :], in0=pb[0][:, F:2 * F], scalar=gate[:, 0:1], in1=sg[:, 0, :],
                                               op0=ALU.mult, op1=ALU.mult).then_inc(act_set, 1)
                        dve.wait_ge(y_ready, j + (2 * NE + 2 + 1))
                        V.tensor_copy(y[:, 0, 0:512], pb[6][:, :]).then_inc(yB_set, 1)
                        V.tensor_copy(y[:, 0, 512:1024], pb[7][:, :]).then_inc(m_y, 1)
            for t in range(TT):
                n_ = rows_of[t]
                dve.wait_ge(rows_in[t % 2], 16 * (t // 2 + 1))
                V.tensor_tensor(y[0:n_, t % 2, :], y[0:n_, t % 2, :], row(3, t, 0, D), ALU.mult).then_inc(y_step, 1)
                dve.wait_ge(y_step, t + 1)
                V.tensor_tensor(x[0:n_, t, :], x[0:n_, t, :], y[0:n_, t % 2, :], ALU.add).then_inc(y_set, 1)

        def scalar_after(act):
            A, C = nc.scalar.activation, nc.scalar.copy
            for n in range(2 * QB):
                t, m = n // 2, n % 2
                act.wait_ge(heads_set, 2 + 2 * NS)
                act.wait_ge(oT_added, 1 + NS)
                if n >= 2:
                    act.wait_ge(squares, SQ0 + n - 1)
                A(junk[:, (n % 2) * W:(n % 2) * W + W], x[:, t, m * W:m * W + W], ACT.Square, accum_out=ss[:, n:n + 1]
                  ).then_inc(squares, 1)
            act.wait_ge(squares, SQ0 + 2 * QB)
            A(ss, ss, ACT.Sqrt, scale=1.0 / W, bias=EPS).then_inc(roots, 1)
            for j in range(8):
                act.wait_ge(rows_ready, j + 1)
                C(RB[:, j // 2, j % 2 * 512:j % 2 * 512 + 512], pb[j % 2][:, :]).then_inc(rows_copied, 1)
            for j in range(8):
                act.wait_ge(rows_ready, 8 + j + 1)
                C(RS[:, j // 2, j % 2 * 512:j % 2 * 512 + 512], pb[2 + j % 2][0:NS, :]).then_inc(rows_copied, 1)
            for c in range(KC):
                act.wait_ge(x_turned, HT0 + c + 1)
                A(hT[:, c, 0:SEQ], pb[4 + c % 2][:, :], ACT.Copy, scale=cgain[:, c, 2:3]).then_inc(hT_set, 1)
            act.wait_ge(oms_ready, 1)
            A(rsx, pb[6][:, 0:2 * NS].rearrange("p (a b) -> p a b", b=NS), ACT.Sqrt, scale=1.0 / W, bias=EPS).then_inc(roots, 1)
            for t in range(TT):
                n_ = rows_of[t]
                act.wait_ge(x1_set, 2 * t + 2)
                if t >= 1:
                    act.wait_ge(squares, SQ0 + 2 * QB + t)
                A(junk[0:n_, :], x[0:n_, t, :], ACT.Square, accum_out=ss[0:n_, t:t + 1]).then_inc(squares, 1)
                act.wait_ge(squares, SQ0 + 2 * QB + t + 1)
                A(ss[0:n_, t:t + 1], ss[0:n_, t:t + 1], ACT.Sqrt, scale=1.0 / D, bias=EPS).then_inc(roots, 1)
                for hh in range(2):
                    act.wait_ge(h2_turned, 2 * t + hh + 1)
                    A(hT[:, hh * 4:hh * 4 + 4, t * P:t * P + n_], pb[4 + hh][:, :].rearrange("p (a b) -> p a b", b=P)[:, :, 0:n_],
                      ACT.Copy).then_inc(h2T_set, 1)
            act.wait_ge(logit_ready, TT)
            act.wait_ge(score_clear, 1)
            A(score[:, 0:QB, :], pb[6][:, 0:QB * NE].rearrange("p (a b) -> p a b", b=NE), ACT.Sigmoid).then_inc(scored, 1)
            A(score[0:NS, QB, :], pb[6][0:NS, QB * NE:TT * NE], ACT.Sigmoid).then_inc(scored, 1)

            def shared_silu(t):
                n_ = rows_of[t]
                act.wait_ge(sgu_ready, t + 1)
                if t >= 2:
                    act.wait_ge(sact_set, t - 1)
                A(sg[0:n_, t % 2, :], pb[t % 2][0:n_, 0:F], ACT.Silu).then_inc(ssg_set, 1)

            shared_silu(0)
            shared_silu(1)
            for t in range(TT):
                n_ = rows_of[t]
                act.wait_ge(sa_turned, t + 1)
                if t >= 2:
                    act.wait_ge(sy_ready, 2 * t - 2)
                C(aT[:, t % 2, :, 0:n_], pb[2][:, 0:2 * P].rearrange("p (a b) -> p a b", b=P)[:, :, 0:n_]).then_inc(saT_set, 1)
                if t + 2 < TT:
                    shared_silu(t + 2)
            act.sem_inc(aT_set, 1)
            act.sem_inc(yA_set, 1)
            act.wait_ge(xg_turned, 1)
            C(xT[:, 0, 0:4, :].rearrange("p a b -> p (a b)"), pb[2][:, :]).then_inc(xTa_set, 1)
            with act.Fori(0, NE // 2) as i:
                for u in range(2):
                    act.wait_ge(gu_ready, i * 2 + (u + 1))
                    act.wait_ge(act_set, i * 2 + (u + 1))
                    A(sg[:, u, :], pb[u][:, 0:F], ACT.Silu).then_inc(sg_set, 1)
                    act.wait_ge(xg_turned, i * 4 + (2 * u + 3))
                    C(xT[:, 1 - u, 0:4, :].rearrange("p a b -> p (a b)"), pb[2][:, :]).then_inc(xTa_set, 1)
                    act.wait_ge(a_turned, i * 2 + (u + 1))
                    C(aT[:, u, :, :].rearrange("p a b -> p (a b)"), pb[4][:, 0:2 * P]).then_inc(aT_set, 1)
                    act.wait_ge(y_ready, i * 4 + (2 * u + 3))
                    act.wait_ge(y_free, i * 2 + (u + 1))
                    C(y[:, u, 0:512], pb[6][:, :]).then_inc(yA_set, 1)
            act.wait_ge(m_over, 1)
            more = act.value_load(over[0:1, 0:1], min_val=0, max_val=OVER)
            with act.If(more > 0):
                with act.Fori(0, more) as i:
                    with act.Fori(0, NE) as e:
                        j = i * NE + e
                        act.wait_ge(gu_ready, j + (NE + 1))
                        A(sg[:, 0, :], pb[0][:, 0:F], ACT.Silu).then_inc(sg_set, 1)
                        act.wait_ge(a_turned, j + (NE + 1))
                        C(aT[:, 0, :, :].rearrange("p a b -> p (a b)"), pb[4][:, 0:2 * P]).then_inc(aT_set, 1)

        def sync_after(sp):
            sp.wait_ge(o8_turned, NS)
            sp.wait_ge(heads_set, 2 + 2 * NS)
            for s in range(2):
                sp.dma_start(wslot[s], I["w_o"][:, s * 512:s * 512 + 512].rearrange("(k p) n -> p k n", p=P)
                             ).then_inc(group_in[s], 16)
            sp.dma_start(xres[:, :], I["x"][0:P, :]).then_inc(xres_in, 16)
            sp.dma_start(wslot[2], I["ws_gate_up"].rearrange("(k p) n -> p k n", p=P)).then_inc(group_in[2], 16)

            def load_gu(u, w):
                sp.dma_start(wgu[u], w.rearrange("(k p) n -> p k n", p=P)).then_inc(wgu_in[u], 16)

            def load_dn(u, w):
                sp.dma_start(wdn[u], w.rearrange("(c p) n -> p c n", p=P)).then_inc(wdn_in[u], 16)

            for e in range(2):
                load_gu(e, I["w_gate_up"][e])
                load_dn(e, I["w_down"][e])
            for t in range(1, TT + 1):
                if t < TT:
                    sp.wait_ge(x1_set, 2 * t)
                    sp.dma_start(xres[0:rows_of[t], :], I["x"][t * P:t * P + rows_of[t], :]).then_inc(xres_in, 16)
                sp.wait_ge(h2_set, t)
                n_ = rows_of[t - 1]
                sp.dma_start(h2d[(t - 1) * P:(t - 1) * P + n_, :], hst[(t - 1) % 2][0:n_, :]
                             ).then_inc(h2_out[(t - 1) % 2], 16)
            sp.wait_ge(proj_ready, 2 * TT)
            sp.dma_start(wsd, I["ws_down"].rearrange("(c p) n -> p c n", p=P)).then_inc(wsd_in, 16)
            with sp.Fori(1, NE // 2) as i:
                for u in range(2):
                    sp.wait_ge(gu_ready, i * 2 + (u - 1))
                    load_gu(u, I["w_gate_up"][ds(i * 2 + u, 1), :, :].rearrange("a k n -> (a k) n"))
                    sp.wait_ge(y_ready, i * 4 + (2 * u))
                    load_dn(u, I["w_down"][ds(i * 2 + u, 1), :, :].rearrange("a k n -> (a k) n"))
            sp.wait_ge(m_over, 1)
            more = sp.value_load(over[0:1, 0:1], min_val=0, max_val=OVER)
            with sp.If(more > 0):
                with sp.Fori(0, more) as i:
                    with sp.Fori(0, NE) as e:
                        j = i * NE + e
                        sp.wait_ge(oh_set, j + (NE + 2 + 1))
                        sp.dma_start(wgu[0], I["w_gate_up"][ds(e, 1), :, :].rearrange("a (k p) n -> (a p) k n", p=P)
                                     ).then_inc(m_in, 16)
                        sp.dma_start(wdn[0], I["w_down"][ds(e, 1), :, :].rearrange("a (c p) n -> (a p) c n", p=P)
                                     ).then_inc(m_in, 16)
            sp.wait_ge(routed_done, 1)
            for t in range(TT):
                n_ = rows_of[t]
                if t >= 2:
                    sp.wait_ge(y_set, t - 1)
                sp.dma_start(y[0:n_, t % 2, :], rsum[t * P:t * P + n_, :]).then_inc(rows_in[t % 2], 16)
                if t >= 1:
                    sp.wait_ge(y_set, t)
                    sp.dma_start(O["y"][(t - 1) * P:t * P, :], x[:, t - 1, :]).then_inc(r_out, 16)
            sp.wait_ge(y_set, TT)
            sp.dma_start(O["y"][SEQ:T, :], x[0:NS, QB, :]).then_inc(r_out, 16)
            sp.wait_ge(r_out, 16 * TT)
            sp.wait_ge(kv_out, 16 * 15)

        def pool_after(pool):
            pool.wait_ge(o8_turned, NS)
            pool.dma_start(wr, I["w_router"]).then_inc(wr_in, 16)
            pool.wait_ge(win_out, 16 * 2 * NS)
            pool.wait_ge(h2_out[0], 16 * 3)
            pool.wait_ge(h2_out[1], 16 * 2)
            pool.wait_ge(xg_clear, 1)

            def gather(u, s):
                nc.gpsimd.indirect_dma_start(xg[:, u, :], None, h2d, bass.IndirectOffsetOnAxis(ap=gidx1[u], axis=0),
                                             bounds_check=T - 1, oob_is_err=False).then_inc(s, 16)

            def scatter(u, idx, s):
                nc.gpsimd.indirect_dma_start(rsum, bass.IndirectOffsetOnAxis(ap=idx, axis=0), y[:, u, :], None,
                                             bounds_check=T + SLOTS - 1, oob_is_err=True, compute_op=ALU.add).then_inc(s, 16)

            for e in range(2):
                pool.wait_ge(gidx_set, e + 1)
                gather(e, xg_in[e])
            pool.sem_inc(y_free, 1)
            with pool.Fori(0, NE // 2) as i:
                for u in range(2):
                    pool.wait_ge(gidx_set, i * 2 + (u + 3))
                    pool.wait_ge(xg_turned, i * 4 + (2 * u + 2))
                    pool.sem_inc(asked, 1)
                    gather(u, xg_in[u])
                    pool.wait_ge(yA_set, i * 2 + (u + 2))
                    pool.wait_ge(yB_set, i * 2 + (u + 2))
                    pool.wait_ge(sidx_set, i * 8 + (4 * u + 7))
                    pool.wait_ge(scattered, i * 32 + 16 * (ZEROS + u))
                    pool.sem_inc(y_free, 1)
                    scatter(u, sidx1[u], scattered)
            pool.wait_ge(scattered, 16 * (ZEROS + NE))
            pool.wait_ge(xg_in[0], 16 * (NE // 2 + 1))
            pool.wait_ge(xg_in[1], 16 * (NE // 2 + 1))
            pool.wait_ge(m_over, 1)
            more = pool.value_load(over[0:1, 0:1], min_val=0, max_val=OVER)
            with pool.If(more > 0):
                with pool.Fori(0, more) as i:
                    with pool.Fori(0, NE) as e:
                        j = i * NE + e
                        pool.wait_ge(gidx_set, j + (NE + 2 + 1))
                        pool.sem_inc(asked, 1)
                        gather(0, xg_in[0])
                        pool.wait_ge(scattered, j * 16 + 16 * (ZEROS + NE))
                        pool.wait_ge(m_y, i * (NE + 1) + (e + 2))
                        pool.sem_inc(asked, 1)
                        scatter(0, gidx1[0], scattered)
            pool.wait_ge(scattered, more * (16 * NE) + 16 * (ZEROS + NE))
            pool.sem_inc(routed_done, 1)

        block = es.enter_context(nc.Block())

        @block.sync
        def _(sp):
            sp.dma_start(cst[:, :], I["consts"]).then_inc(small_in, 16)
            sp.dma_start(cT, I["c_cols"]).then_inc(c_in, 16)

            def load_group(s, src):
                sp.dma_start(wslot[s], src.rearrange("(k p) n -> p k n", p=P)).then_inc(group_in[s], 16)

            load_group(0, I["w_ada"][:, 0:512])
            sp.dma_start(cgain[:, :, 0:3], I["gains"]).then_inc(small_in, 16)
            sp.dma_start(gqk, I["g_qk"]).then_inc(small_in, 16)
            sp.dma_start(bada, I["b_ada"]).then_inc(small_in, 16)
            sp.dma_start(bfc, I["b_f"]).then_inc(small_in, 16)
            sp.dma_start(ebs, I["e_bias"]).then_inc(small_in, 16)
            sp.dma_start(wf, I["w_in"][:, 3 * W:3 * W + H].rearrange("(k p) n -> p k n", p=P)).then_inc(small_in, 16)
            sp.dma_start(ptab[:, :], I["pages"]).then_inc(ptab_in, 16)
            for s in (1, 2):
                load_group(s, I["w_ada"][:, 512 * s:512 * s + 512])
            for t in range(QB):
                sp.dma_start(x[:, t, :], I["x"][t * P:t * P + P, :]).then_inc(x_in, 16)
            sp.dma_start(x[0:NS, QB, :], I["x"][SEQ:T, :]).then_inc(x_in, 16)
            with sp.Fori(1, 4) as i:
                for s in range(3):
                    sp.wait_ge(group_used, i * 3 + (s - 2))
                    load_group(s, I["w_ada"][:, ds(i * 1536 + s * 512, 512)])
            for g, s in ring:
                sp.wait_ge(group_used, g - 2)
                load_group(s, I["w_in"][:, win_cols[g - 12]:win_cols[g - 12] + 512])
            sp.wait_ge(ptab_in, 16)

            def load_k(b, ch):
                sp.wait_ge(k_scored, b * NCH + (ch + 1))
                for n in range(CH):
                    page = sp.value_load(ptab[0:1, ds(b * PAGES + (ch * CH + n), 1)], min_val=0, max_val=NPHYS - 1)
                    sp.dma_start(kring[:, ch % 2, n, :, :],
                                 I["cache_k"][ds(page, 1), :, :, :].rearrange("a p c t -> (a p) c t")
                                 ).then_inc(k_in[ch % 2], 16)

            sp.wait_ge(v_ready, 2 * TT)
            with sp.Fori(0, NS // 2) as i:
                for u in range(2):
                    b = i * 2 + u
                    load_k(b, 0)
                    load_k(b, 1)
                    sp.wait_ge(w_scored, i * 2 + (u + 1))
                    sp.dma_start(wink[u], I["win_k_seen"][ds(b, 1), :, :, :].rearrange("a p c t -> (a p) c t")
                                 ).then_inc(wink_in[u], 16)
                    sp.wait_ge(sA_step, i * 2 * NCH + (u * NCH + 1))
                    sp.wait_ge(suffix_out, 16)
                    sp.dma_start(suffix, lfr[ds(b * PAGES, PAGES), :, :].rearrange("g h t -> h g t")
                                 ).then_inc(suffix_in, 16)
                    load_k(b, 2)
                    load_k(b, 3)
            sync_after(sp)

        @block.gpsimd
        def _(pool):
            pool.dma_start(pidx[:, :], I["page_rows"]).then_inc(pidx_in, 16)
            nc.gpsimd.memset(zero, 0.0).then_inc(zero_set, 1)
            pool.wait_ge(zero_set, 1)
            for t in range(-(-(T + SLOTS) // P)):
                n = min(P, T + SLOTS - t * P)
                for c in range(2):
                    pool.dma_start(rsum[t * P:t * P + n, c * 512:c * 512 + 512].rearrange("p (a b) -> p a b", a=8),
                                   zero[0:n, :].unsqueeze(1).broadcast_to([n, 8, 64])).then_inc(scattered, 16)
            pool.wait_ge(pidx_in, 16)
            pool.wait_ge(x_turned, KC + 1)
            nc.gpsimd.indirect_dma_start(
                lfc.rearrange("p a b -> p (a b)"), None, I["cache_lf"].rearrange("g h t -> g (h t)"),
                bass.IndirectOffsetOnAxis(ap=pidx[:, 0:1], axis=0),
                bounds_check=NPHYS - 1, oob_is_err=True).then_inc(lfc_in, 16)

            def copy_window(name, out, b):
                rows = (PAST - 1) * W
                pool.dma_start(
                    O[out][b, 0:PAST - 1, :].rearrange("r c -> (r c)").rearrange("(a n) -> a n", n=rows // 16),
                    I[name][b, 1:PAST, :].rearrange("r c -> (r c)").rearrange("(a n) -> a n", n=rows // 16)
                ).then_inc(win_out, 16)

            for b in range(NS):
                pool.wait_ge(raw_ready, 2 * b + 1)
                copy_window("win_k", "win_k_s", b)
            pool.wait_ge(ptab_in, 16)

            def load_v(b, ch):
                pool.wait_ge(v_used, b * NCH + (ch + 1))
                for n in range(CH):
                    page = pool.value_load(ptab[0:1, ds(b * PAGES + (ch * CH + n), 1)], min_val=0, max_val=NPHYS - 1)
                    pool.dma_start(vring[:, ch % 2, n, :],
                                   I["cache_v"][ds(page, 1), :, :].rearrange("a t c -> (a t) c")
                                   ).then_inc(v_in[ch % 2], 16)

            pool.wait_ge(scattered, 16 * ZEROS)
            pool.wait_ge(v_ready, 2 * TT)
            with pool.Fori(0, NS // 2) as i:
                for u in range(2):
                    b = i * 2 + u
                    load_v(b, 0)
                    load_v(b, 1)
                    pool.wait_ge(oB_ready, i * 2 + (u + 1))
                    pool.dma_start(winv[u], I["win_v_seen"][ds(b, 1), :, :, :].rearrange("a p s c -> (a p) s c")
                                   ).then_inc(winv_in[u], 16)
                    load_v(b, 2)
                    load_v(b, 3)
                    rows = (PAST - 1) * W
                    pool.dma_start(
                        O["win_v_s"][ds(b, 1), 0:PAST - 1, :].rearrange("z r c -> (z r c)").rearrange("(a n) -> a n", n=rows // 16),
                        I["win_v"][ds(b, 1), 1:PAST, :].rearrange("z r c -> (z r c)").rearrange("(a n) -> a n", n=rows // 16)
                    ).then_inc(win_out, 16)
            pool_after(pool)

        @block.tensor
        def _(pe):
            mm, turn = nc.tensor.matmul, nc.tensor.transpose
            pe.wait_ge(silu_c, 1)
            with pe.Fori(0, 4) as i:
                for s in range(3):
                    pe.wait_ge(group_in[s], i * 16 + 16)
                    for blk in range(4):
                        for k in range(KC):
                            last = mm(pb[6][:, ds(i * (12 * 9) + (s * 4 + blk) * 9, 9)],
                                      lhsT=wslot[s][:, k, blk * P:blk * P + P], rhs=sT[:, k, :],
                                      start=(k == 0), stop=(k == KC - 1))
                    last.then_inc(group_used, 1)
            for c in range(KC):
                if c >= 2:
                    pe.wait_ge(hT_set, c - 1)
                for t in range(QB):
                    if c == 0:
                        pe.wait_ge(x_scaled, t + 1)
                    last = turn(pb[c % 2][:, t * P:t * P + P], x[:, t, c * P:c * P + P], ident)
                last.then_inc(x_turned, 1)
            pe.wait_ge(x_scaled, TT)
            for c in range(KC):
                last = turn(pb[7][:, c * NS:c * NS + NS], x[0:NS, QB, c * P:c * P + P], ident[0:NS, 0:NS])
            last.then_inc(x_turned, 1)

            def mean_square(n):
                pe.wait_ge(sq_ready, n + 1)
                if n >= 2:
                    pe.wait_ge(rms_ready, n - 1)
                mm(pb[2 + n % 2][:, :], lhsT=headmean, rhs=sq[:, n % 2, :], start=True, stop=True).then_inc(ms_ready, 1)

            def rotation(n):
                if n < 2 * NP:
                    return
                pe.wait_ge(qk_set, n + 1)
                if n >= 2 * NP + 2:
                    pe.wait_ge(rope_set, n - 2 * NP - 1)
                mm(pb[4 + n % 2][:, :], lhsT=rotate, rhs=qkT[:, n, 0:SEQ], start=True, stop=True).then_inc(rot_ready, 1)

            pe.wait_ge(hT_set, KC + 1)
            for n in range(QKC):
                g, s = ring[n // 4]
                if n % 4 == 0:
                    pe.wait_ge(group_in[s], 16 * (g // 3 + 1))
                if n >= 2:
                    pe.wait_ge(qk_set, n - 1)
                for k in range(KC):
                    w = wslot[s][:, k, n % 4 * P:n % 4 * P + P]
                    last = mm(pb[n % 2][:, :], lhsT=w, rhs=hT[:, k, 0:SEQ], start=(k == 0), stop=(k == KC - 1))
                last.then_inc(raw_ready, 1)
                for k in range(KC):
                    w = wslot[s][:, k, n % 4 * P:n % 4 * P + P]
                    last = mm(pb[7][:, n * NS:n * NS + NS], lhsT=w, rhs=hT[:, k, SEQ:T], start=(k == 0), stop=(k == KC - 1))
                if n % 4 == 3:
                    last.then_inc(group_used, 1)
                if n >= 1:
                    mean_square(n - 1)
                if n >= 2:
                    rotation(n - 2)
            for n in range(2 * TT):
                m, t = n // TT, n % TT
                g, s = ring[4 + m]
                rows = P if t < QB else NS
                if t == 0:
                    pe.wait_ge(group_in[s], 16 * (g // 3 + 1))
                if n < 2:
                    pe.wait_ge(qk_set, QKC - 1 + n)
                else:
                    pe.wait_ge(v_copied, n - 1)
                for k in range(KC):
                    last = mm(pb[n % 2][0:rows, :], lhsT=hT[:, k, t * P:t * P + rows], rhs=wslot[s][:, k, :],
                              start=(k == 0), stop=(k == KC - 1))
                last.then_inc(v_ready, 1)
                if n == 0:
                    mean_square(QKC - 1)
                    rotation(QKC - 2)
                if n == 1:
                    rotation(QKC - 1)
            pe.wait_ge(rms_ready, QKC)
            for k in range(KC):
                mm(pb[3][0:H, :], lhsT=wf[:, k, :], rhs=hT[:, k, 0:SEQ], start=(k == 0), stop=(k == KC - 1))
            for k in range(KC):
                last = mm(pb[2][0:H, 0:NS], lhsT=wf[:, k, :], rhs=hT[:, k, SEQ:T], start=(k == 0), stop=(k == KC - 1))
            last.then_inc(f_ready, 1)
            pe.wait_ge(sq_ready, QKC + 1)
            pe.wait_ge(rope_set, 2 * NP)
            mm(pb[4][:, 0:QKC * NS], lhsT=headmean, rhs=sqS.rearrange("p a b -> p (a b)"), start=True, stop=True
               ).then_inc(ms_ready, 1)
            pe.wait_ge(qk_set, QKC + 1)
            mm(pb[5][:, 0:2 * NP * NS], lhsT=rotate, rhs=qkT[:, 2 * NP:, SEQ:T], start=True, stop=True
               ).then_inc(rot_ready, 1)
            pe.wait_ge(lfc_scanned, 1)
            mm(pb[6][:, 0:H], lhsT=laterpg, rhs=ptot, start=True, stop=True).then_inc(later_ready, 1)
            pe.wait_ge(cum_set, 1)
            for t in range(QB):
                last = turn(pb[3][:, t * H:t * H + H], cum[:, t * P:t * P + P], ident[0:H, 0:H])
            last.then_inc(cols_turned, 1)
            pe.wait_ge(rope_set, 2 * NP + 1)
            for c in range(NP):
                last = turn(pb[4][0:NS, c * P:c * P + P], qkT[:, 3 * NP + c, SEQ:T], ident)
            last.then_inc(knew_turned, 1)

            pe.sem_inc(k_scored, 2)
            pe.sem_inc(v_used, 2)
            pe.sem_inc(w_scored, 2)
            pe.sem_inc(oB_ready, 2)
            pe.wait_ge(cols_set, 1)
            pe.wait_ge(knew_set, 1)
            pe.wait_ge(v_copied, 2 * TT)
            with pe.Fori(0, NS // 2) as i:
                for u in range(2):
                    b = i * 2 + u
                    pe.wait_ge(q_split, i * 2 + (u + 1))
                    pe.wait_ge(o8_set, i * 4 + (2 * u + 2))
                    for ch in range(NCH):
                        pe.wait_ge(k_in[ch % 2], i * 256 + (u * 128 + 64 * (ch // 2 + 1)))
                        if ch >= 2:
                            pe.wait_ge(sA_step, i * 2 * NCH + (u * NCH + 1 + ch - 1))
                        for pr in range(NP):
                            last = mm(pb[ch % 2][0:H, :], lhsT=ksel[:, 0, pr, :], rhs=kring[:, ch % 2, :, pr, :],
                                      start=(pr == 0), stop=(pr == NP - 1))
                        last.then_inc(k_scored, 1)
                    pe.wait_ge(wink_in[u], i * 16 + 16)
                    pe.wait_ge(pB_copied, i * 2 + (u + 1))
                    for pr in range(NP):
                        mm(pb[2][0:H, 0:WK], lhsT=ksel[:, 1, pr, :], rhs=wink[u][:, pr, :],
                           start=(pr == 0), stop=(pr == NP - 1))
                    for pr in range(NP):
                        mm(pb[2][0:H, WK:WK + NS], lhsT=ksel[:, 1, pr, :], rhs=qkT[:, 3 * NP + pr, SEQ:T],
                           start=(pr == 0), stop=(pr == NP - 1))
                    for pr in range(NP):
                        last = mm(pb[2][0:H, WK + NS:WK + 2 * NS], lhsT=ksel[:, 0, pr, :], rhs=qkT[:, NP + pr, SEQ:T],
                                  start=(pr == 0), stop=(pr == NP - 1))
                    last.then_inc(w_scored, 1)
                    pe.wait_ge(cumh_set, i * 2 + (u + 1))
                    pe.wait_ge(p_copied, i * 16 + (8 * u + 1))
                    mm(pb[6][:, :], lhsT=ones[0:H, :], rhs=cumh, start=True, stop=True).then_inc(decay_ready, 1)

                    def scores(n):
                        m, q = n // QB, n % QB
                        nk = (q + 1) * P
                        if n == 0:
                            pe.wait_ge(staged, i + 1)
                        pe.wait_ge(s_set, i * 16 + (8 * u + n + 1))
                        mm(pb[3 + n % 2][:, 0:nk], lhsT=stage[u * DH:u * DH + DH, 2 * m, q * P:q * P + P],
                           rhs=stage[u * DH:u * DH + DH, 2 * m + 1, 0:nk], start=True, stop=True).then_inc(s_ready, 1)

                    def turn_p(n):
                        q = n % QB
                        pe.wait_ge(p_ready, i * 16 + (8 * u + n + 1))
                        if n == 0:
                            pe.wait_ge(decay_set, i * 2 + (u + 1))
                        else:
                            pe.wait_ge(p_copied, i * 16 + (8 * u + n + 1))
                        for j in range(q + 1):
                            last = turn(pb[6][:, j * P:j * P + P], sx[:, n % 2, j * P:j * P + P], ident)
                        last.then_inc(p_turned, 1)

                    def values(n):
                        m, q = n // QB, n % QB
                        if n == 0:
                            pe.wait_ge(heads_set, i * 4 + (2 * u + 2))
                        pe.wait_ge(p_copied, i * 16 + (8 * u + n + 2))
                        for j in range(q + 1):
                            last = mm(pb[7][:, n * DH:n * DH + DH], lhsT=pT[:, n % 2, j, :],
                                      rhs=v[:, j, ds(i * 2 * DH + (u * DH + m * W), DH)], start=(j == 0), stop=(j == q))
                        return last

                    for n in range(2 * QB + 2):
                        if n < 2 * QB:
                            scores(n)
                        if n >= 2:
                            last = values(n - 2)
                            if n - 2 == 2 * QB - 1:
                                last.then_inc(pv_ready, 1)
                        if 1 <= n <= 2 * QB:
                            turn_p(n - 1)

                    pe.wait_ge(small_in, 16 * 7)
                    pe.wait_ge(pA_ready, i * 2 + (u + 1))
                    pe.wait_ge(oT_added, i * 2 + (u + 1))
                    for g in range(PAGES):
                        turn(pb[5][:, g * H:g * H + H], sA[:, g * PAGE:g * PAGE + PAGE], ident[0:H, 0:H])
                    turn(pb[5][0:NS, PAGES * H:PAGES * H + H], sA[:, PAST:PAST + NS], ident[0:H, 0:H]).then_inc(pA_turned, 1)
                    pe.wait_ge(small_in, 16 * 7)
                    pe.wait_ge(pB_ready, i * 2 + (u + 1))
                    for g in range(3):
                        turn(pb[2][:, g * H:g * H + H], sB[:, g * P:g * P + P], ident[0:H, 0:H])
                    turn(pb[2][0:NS, 3 * H:4 * H], sB[:, WK:WK + NS], ident[0:H, 0:H]).then_inc(pB_turned, 1)
                    pe.wait_ge(pA_copied, i * 2 + (u + 1))
                    for ch in range(NCH):
                        pe.wait_ge(v_in[ch % 2], i * 256 + (u * 128 + 64 * (ch // 2 + 1)))
                        for n in range(CH):
                            last = mm(pb[0][0:H, :], lhsT=pdA[:, ch * CH + n, :], rhs=vring[:, ch % 2, n, :],
                                      start=(ch + n == 0), stop=False)
                        last.then_inc(v_used, 1)
                    mm(pb[0][0:H, :], lhsT=pdo[:, 0, :], rhs=v[0:NS, QB, 0:W], start=False, stop=True)
                    pe.wait_ge(winv_in[u], i * 16 + 16)
                    pe.wait_ge(pB_copied, i * 2 + (u + 2))
                    for g in range(3):
                        mm(pb[1][0:H, :], lhsT=pdB[:, g, :], rhs=winv[u][:, g, :], start=(g == 0), stop=False)
                    mm(pb[1][0:H, :], lhsT=pdo[:, 1, :], rhs=v[0:NS, QB, W:2 * W], start=False, stop=True
                       ).then_inc(oB_ready, 1)
                    for m in range(2):
                        pe.wait_ge(o8_set, i * 4 + (2 * u + m + 3))
                        for c in range(NP):
                            last = mm(pb[5][:, (m * NP + c) * H:(m * NP + c) * H + H], lhsT=o8[:, m, c * P:c * P + P],
                                      rhs=ident[0:H, 0:H], start=True, stop=True)
                    last.then_inc(o8_turned, 1)
            tensor_after(pe)

        @block.vector
        def _(dve):
            V = nc.vector
            dve.wait_ge(small_in, 16 * 7)
            dve.wait_ge(c_in, 16)
            dve.wait_ge(sig_c, 1)
            V.tensor_tensor(sT, cT, sT, ALU.mult).then_inc(silu_c, 1)
            V.tensor_scalar(gsc[:, 0:4:2], gqk[:, 0:4:2], SCALE, None, ALU.mult).then_inc(gains_set, 1)
            V.tensor_copy(gsc[:, 1:4:2], gqk[:, 1:4:2]).then_inc(gains_set, 1)
            dve.wait_ge(roots, 1)
            V.reciprocal(rs[:, 0:QB], ss[:, 0:QB]).then_inc(inverses, 1)
            V.reciprocal(rs[0:NS, QB:TT], ss[0:NS, QB:TT]).then_inc(inverses, 1)
            dve.wait_ge(inverses, 2)
            for t in range(TT):
                n = P if t < QB else NS
                V.tensor_scalar(x[0:n, t, :], x[0:n, t, :], rs[0:n, t:t + 1], None, ALU.mult).then_inc(x_scaled, 1)
            dve.wait_ge(group_used, 12)
            V.tensor_tensor(mod, pb[6][:, 0:6 * KC * 9].rearrange("p (a b) -> p a b", b=9),
                            bada.unsqueeze(2).broadcast_to([P, 6 * KC, 9]), ALU.add).then_inc(mod_set, 1)
            dve.wait_ge(mod_set, 1)
            for n, k in enumerate((1, 4)):
                V.scalar_tensor_tensor(out=mod[:, k * KC:k * KC + KC, :], in0=mod[:, k * KC:k * KC + KC, :], scalar=1.0,
                                       in1=cgain[:, :, n:n + 1].broadcast_to([P, KC, 9]),
                                       op0=ALU.add, op1=ALU.mult).then_inc(mod_set, 1)
            dve.wait_ge(mod_set, 3)
            for c in range(KC):
                dve.wait_ge(x_turned, c + 1)
                V.tensor_scalar(hT[:, c, 0:SEQ], pb[c % 2][:, :], mod[:, KC + c, 0:1], mod[:, c, 0:1],
                                ALU.mult, ALU.add).then_inc(hT_set, 1)
            dve.wait_ge(x_turned, KC + 1)
            V.tensor_tensor(hT[:, :, SEQ:T], pb[7][:, 0:KC * NS].rearrange("p (a b) -> p a b", b=NS),
                            mod[:, KC:2 * KC, 1:9], ALU.mult).then_inc(mod_set, 1)
            dve.wait_ge(mod_set, 4)
            V.tensor_tensor(hT[:, :, SEQ:T], hT[:, :, SEQ:T], mod[:, 0:KC, 1:9], ALU.add).then_inc(hT_set, 1)
            steps = 0
            for n in range(QKC):
                dve.wait_ge(rms_ready, n + 1)
                V.reciprocal(rr[:, n % 2, :], rr[:, n % 2, :]).then_inc(rr_set, 1)
                dve.wait_ge(rr_set, n + 1)
                V.scalar_tensor_tensor(out=qkT[:, n, 0:SEQ], in0=pb[n % 2][:, :], scalar=gsc[:, n // NP:n // NP + 1],
                                       in1=rr[:, n % 2, :], op0=ALU.mult, op1=ALU.mult).then_inc(qk_set, 1)
                if n >= 2 * NP:
                    dve.wait_ge(qk_set, n + 1)
                    if n > 2 * NP:
                        dve.wait_ge(rope_set, n - 2 * NP)
                    V.tensor_tensor(rope1, qkT[:, n, 0:SEQ], cst[:, C_COS:C_COS + SEQ], ALU.mult).then_inc(rope_step, 1)
                    dve.wait_ge(rot_ready, n - 2 * NP + 1)
                    V.tensor_tensor(rope2, pb[4 + n % 2][:, :], cst[:, C_SIN:C_SIN + SEQ], ALU.mult).then_inc(rope_step, 1)
                    steps += 2
                    dve.wait_ge(rope_step, steps)
                    V.tensor_tensor(qkT[:, n, 0:SEQ], rope1, rope2, ALU.add).then_inc(rope_set, 1)
            dve.wait_ge(rms_ready, QKC + 1)
            V.reciprocal(rrS, rrS).then_inc(rr_set, 1)
            dve.wait_ge(rr_set, QKC + 1)
            for g in range(4):
                last = V.scalar_tensor_tensor(
                    out=qkT[:, g * NP:g * NP + NP, SEQ:T],
                    in0=pb[7][:, g * NP * NS:(g + 1) * NP * NS].rearrange("p (a b) -> p a b", b=NS),
                    scalar=gsc[:, g:g + 1], in1=rrS[:, g * NP:g * NP + NP, :], op0=ALU.mult, op1=ALU.mult)
                last.then_inc(rope_step if g < 3 else qk_set, 1)
            dve.wait_ge(qk_set, QKC + 1)
            dve.wait_ge(rope_step, steps + 3)
            V.tensor_scalar(ropeS, qkT[:, 2 * NP:, SEQ:T], cst[:, C_COS + SEQ:C_COS + SEQ + 1], None, ALU.mult
                            ).then_inc(rope_step, 1)
            dve.wait_ge(rope_step, steps + 4)
            dve.wait_ge(rot_ready, 2 * NP + 1)
            V.scalar_tensor_tensor(out=qkT[:, 2 * NP:, SEQ:T],
                                   in0=pb[5][:, 0:2 * NP * NS].rearrange("p (a b) -> p a b", b=NS),
                                   scalar=cst[:, C_SIN + SEQ:C_SIN + SEQ + 1], in1=ropeS, op0=ALU.mult, op1=ALU.add
                                   ).then_inc(rope_set, 1)
            dve.wait_ge(f_ready, 1)
            dve.wait_ge(rope_set, 2 * NP + 1)
            V.tensor_scalar(lfs[:, 0:SEQ], pb[3][0:H, :], bfc, None, ALU.add).then_inc(lf_dve, 1)
            V.tensor_scalar(lfs[:, SEQ:T], pb[2][0:H, 0:NS], bfc, None, ALU.add).then_inc(lf_dve, 1)
            dve.wait_ge(lf_act, 2)
            V.tensor_scalar(lft[:, 2, :], lft[:, 1, :], 1.0, None, ALU.add).then_inc(lf_dve, 1)
            dve.wait_ge(lf_act, 3)
            V.tensor_scalar(lft[:, 2, :], lft[:, 2, :], -1.0, 2.0 ** -24, ALU.add, ALU.max).then_inc(lf_dve, 1)
            dve.wait_ge(lf_dve, 4)
            V.reciprocal(lft[:, 4, :], lft[:, 2, :]).then_inc(lf_dve, 1)
            dve.wait_ge(lf_dve, 5)
            V.tensor_tensor(lft[:, 4, :], lft[:, 4, :], lft[:, 1, :], ALU.mult).then_inc(lf_dve, 1)
            dve.wait_ge(lf_dve, 6)
            V.tensor_tensor(lft[:, 3, :], lft[:, 4, :], lft[:, 3, :], ALU.mult).then_inc(lf_dve, 1)
            V.scalar_tensor_tensor(out=lft[:, 0, :], in0=lft[:, 2, :], scalar=2.0 ** -23, in1=lft[:, 1, :],
                                   op0=ALU.is_lt, op1=ALU.mult).then_inc(lf_dve, 1)
            dve.wait_ge(lf_dve, 8)
            V.tensor_tensor(lft[:, 3, :], lft[:, 3, :], lft[:, 0, :], ALU.add).then_inc(lf_dve, 1)
            dve.wait_ge(lf_dve, 9)
            V.scalar_tensor_tensor(out=lfs[:, :], in0=lfs[:, :], scalar=0.0, in1=lft[:, 3, :],
                                   op0=ALU.min, op1=ALU.subtract).then_inc(lf_dve, 1)
            dve.wait_ge(lf_dve, 10)
            V.memset(cumh, 1.0).then_inc(lf_dve, 1)
            dve.wait_ge(lf_dve, 11)
            V.tensor_tensor_scan(cum, cumh, lfs[:, 0:SEQ], 0.0, ALU.mult, ALU.add).then_inc(cum_set, 1)
            dve.wait_ge(lfc_in, 16)
            for h in range(H):
                last = V.tensor_tensor_scan(lfi[:, h, :], ones, lfc[:, h, :], 0.0, ALU.mult, ALU.add)
                last.then_inc(lf_dve, 1)
            dve.wait_ge(lf_dve, 11 + H)
            V.tensor_copy(ptot, lfi[:, :, PAGE - 1]).then_inc(lfc_scanned, 1)
            dve.wait_ge(later_ready, 1)
            V.tensor_copy(tot, pb[6][:, 0:H]).then_inc(lf_dve, 1)
            dve.wait_ge(lf_dve, 12 + H)
            V.tensor_tensor(lfc[:, :, 1:PAGE], lfi[:, :, 0:PAGE - 1],
                            tot.unsqueeze(2).broadcast_to([P, H, PAGE - 1]), ALU.add).then_inc(suffix_set, 1)
            V.tensor_copy(lfc[:, :, 0], tot).then_inc(suffix_set, 1)
            dve.wait_ge(cols_turned, 1)
            V.tensor_copy(ccol, pb[3][:, 0:QB * H].rearrange("p (a b) -> p a b", b=H)).then_inc(cols_set, 1)
            dve.wait_ge(knew_turned, 1)
            V.tensor_copy(knew, pb[4][0:NS, :]).then_inc(knew_set, 1)

            pick = cst[:, C_PICK:C_PICK + NP * H].rearrange("p (a b) -> p a b", b=H)
            dve.wait_ge(cum_set, 1)
            dve.wait_ge(cols_set, 1)
            dve.wait_ge(kv_out, 16 * 15)
            dve.wait_ge(suffix_out, 16)
            for s, n in ((sA_step, 1), (sB_step, 1), (o8_set, 2), (oT_added, 1), (s_set, 2), (heads_set, 2)):
                dve.sem_inc(s, n)
            with dve.Fori(0, NS // 2) as i:
                for u in range(2):
                    b = i * 2 + u
                    dve.wait_ge(w_scored, i * 2 + (u + 2))
                    for m in range(2):
                        last = V.tensor_tensor(
                            ksel[:, m, :, :], pick,
                            qkT[:, 2 * m * NP:2 * m * NP + NP, ds(i * 2 + (SEQ + u), 1)].broadcast_to([P, NP, H]), ALU.mult)
                        last.then_inc(q_split if m else o8_step, 1)
                    V.tensor_scalar(cumh, cum, cst[0:H, ds(i * 2 + (C_ROW + u), 1)], -1.0, ALU.mult, ALU.mult
                                    ).then_inc(cumh_set, 1)
                    dve.wait_ge(suffix_in, i * 32 + (16 * u + 16))
                    for ch in range(NCH):
                        dve.wait_ge(k_scored, i * 8 + (4 * u + ch + 3))
                        V.scalar_tensor_tensor(out=sA[:, ch * CKEYS:(ch + 1) * CKEYS], in0=pb[ch % 2][0:H, :],
                                               scalar=lfs[:, ds(i * 2 + (SEQ + u), 1)],
                                               in1=suffix[:, ch * CH:ch * CH + CH, :].rearrange("p a b -> p (a b)"),
                                               op0=ALU.add, op1=ALU.add).then_inc(sA_step, 1)
                    dve.wait_ge(w_scored, i * 2 + (u + 3))
                    V.tensor_copy(sB[:, 0:WK], pb[2][0:H, 0:WK]).then_inc(sB_step, 1)
                    V.tensor_tensor(sB[:, WK:], pb[2][0:H, WK:WK + NS],
                                    cst[0:H, ds(i * 2 * NS + (C_OWNB + u * NS), NS)], ALU.add).then_inc(sB_step, 1)
                    V.tensor_tensor(sA[:, PAST:], pb[2][0:H, WK + NS:WK + 2 * NS],
                                    cst[0:H, ds(i * 2 * NS + (C_OWNA + u * NS), NS)], ALU.add).then_inc(sB_step, 1)
                    dve.wait_ge(sA_step, i * 8 + (4 * u + 5))
                    dve.wait_ge(sB_step, i * 6 + (3 * u + 4))
                    V.reduce_max(dnm[:, 0:1], sA, AX.X, negate=True).then_inc(sA_max, 1)
                    V.reduce_max(dnm[:, 1:2], sB, AX.X, negate=True).then_inc(sB_max, 1)
                    for n in range(2 * QB):
                        m, q = n // QB, n % QB
                        nk = (q + 1) * P
                        dst, src = sx[:, n % 2, 0:nk], pb[3 + n % 2][:, 0:nk]
                        if n == 0:
                            dve.wait_ge(decay_set, i * 2 + (u + 1))
                        dve.wait_ge(s_ready, i * 16 + (8 * u + n + 1))
                        dve.wait_ge(p_turned, i * 16 + (8 * u + n - 1)) if n >= 2 else None
                        if m == 0:
                            V.scalar_tensor_tensor(out=dst, in0=src, scalar=ccol[:, q, ds(i * 2 + u, 1)], in1=decay[:, 0:nk],
                                                   op0=ALU.add, op1=ALU.add).then_inc(s_step, 1)
                            dve.wait_ge(s_step, i * 24 + (12 * u + 2 * n + 1))
                            V.tensor_tensor(sx[:, n % 2, q * P:nk], sx[:, n % 2, q * P:nk], tri, ALU.add).then_inc(s_step, 1)
                            dve.wait_ge(s_step, i * 24 + (12 * u + 2 * n + 2))
                        else:
                            V.tensor_tensor(dst, src, cst[:, C_DIL + SEQ - nk:C_DIL + SEQ], ALU.add).then_inc(s_step, 1)
                            dve.wait_ge(s_step, i * 24 + (12 * u + QB + n + 1))
                        V.reduce_max(nm[:, m, q:q + 1], dst, AX.X, negate=True).then_inc(s_set, 1)
                    dve.wait_ge(p_ready, i * 16 + (8 * u + 8))
                    V.reciprocal(rl, lsum).then_inc(rl_set, 1)
                    dve.wait_ge(rl_set, i * 2 + (u + 1))
                    dve.wait_ge(pv_ready, i * 2 + (u + 1))
                    for m in range(2):
                        V.tensor_tensor(x[:, 0:QB, ds(i * 2 * DH + (u * DH + m * W), DH)],
                                        pb[7][:, m * QB * DH:(m + 1) * QB * DH].rearrange("p (a b) -> p a b", b=DH),
                                        rl[:, m, :].unsqueeze(2).broadcast_to([P, QB, DH]), ALU.mult).then_inc(heads_set, 1)
                    dve.wait_ge(pA_ready, i * 2 + (u + 1))
                    dve.wait_ge(pB_ready, i * 2 + (u + 1))
                    V.reciprocal(drl, dls).then_inc(dl_set, 1)
                    dve.wait_ge(dl_set, i * 2 + (u + 1))
                    dve.wait_ge(oB_ready, i * 2 + (u + 3))
                    for m in range(2):
                        V.tensor_scalar(o8[:, m, :], pb[m][0:H, :], drl[:, m:m + 1], None, ALU.mult).then_inc(o8_set, 1)
                    dve.wait_ge(o8_turned, i * 2 + (u + 1))
                    for m in range(2):
                        V.tensor_tensor(otmp, pb[5][:, m * NP * H:(m + 1) * NP * H].rearrange("p (a b) -> p a b", b=H),
                                        pick, ALU.mult).then_inc(o8_step, 1)
                        dve.wait_ge(o8_step, i * 8 + (4 * u + 2 + 2 * m))
                        V.reduce_sum(hT[:, m * NP:m * NP + NP, ds(i * 2 + (SEQ + u), 1)].rearrange("p a b -> p (a b)"), otmp, AX.X
                                     ).then_inc(oT_added if m else o8_step, 1)
                        if m == 0:
                            dve.wait_ge(o8_step, i * 8 + (4 * u + 3))
            vector_after(dve)

        @block.scalar
        def _(act):
            A = nc.scalar.activation
            act.wait_ge(c_in, 16)
            A(sT, cT, ACT.Sigmoid).then_inc(sig_c, 1)
            for t in range(TT):
                n = P if t < QB else NS
                act.wait_ge(x_in, 16 * TT)
                if t >= 2:
                    act.wait_ge(squares, t - 1)
                A(reg_s[0:n, 4096 - 1024 * (t % 2):4096 - 1024 * (t % 2) + D], x[0:n, t, :], ACT.Square,
                  accum_out=ss[0:n, t:t + 1]).then_inc(squares, 1)
            act.wait_ge(squares, TT)
            A(ss[:, 0:QB], ss[:, 0:QB], ACT.Sqrt, scale=1.0 / D, bias=EPS).then_inc(squares, 1)
            A(ss[0:NS, QB:TT], ss[0:NS, QB:TT], ACT.Sqrt, scale=1.0 / D, bias=EPS).then_inc(roots, 1)

            def square(n):
                act.wait_ge(raw_ready, n + 1)
                if n >= 2:
                    act.wait_ge(ms_ready, n - 1)
                A(sq[:, n % 2, :], pb[n % 2][:, :], ACT.Square).then_inc(sq_ready, 1)

            square(0)
            for n in range(QKC):
                if n + 1 < QKC:
                    square(n + 1)
                act.wait_ge(ms_ready, n + 1)
                if n >= 2:
                    act.wait_ge(qk_set, n - 1)
                A(rr[:, n % 2, :], pb[2 + n % 2][:, :], ACT.Sqrt, bias=EPS).then_inc(rms_ready, 1)
            for n in range(2 * TT):
                m, t = n // TT, n % TT
                rows = P if t < QB else NS
                act.wait_ge(v_ready, n + 1)
                A(v[0:rows, t, m * W:m * W + W], pb[n % 2][0:rows, :], ACT.Copy).then_inc(v_copied, 1)
            act.wait_ge(f_ready, 1)
            A(sqS, pb[7][:, 0:QKC * NS].rearrange("p (a b) -> p a b", b=NS), ACT.Square).then_inc(sq_ready, 1)
            act.wait_ge(ms_ready, QKC + 1)
            A(rrS, pb[4][:, 0:QKC * NS].rearrange("p (a b) -> p a b", b=NS), ACT.Sqrt, bias=EPS).then_inc(rms_ready, 1)
            act.wait_ge(lf_dve, 2)
            A(lft[:, 0, :], lfs[:, :], ACT.Abs).then_inc(lf_act, 1)
            act.wait_ge(lf_act, 1)
            A(lft[:, 1, :], lft[:, 0, :], ACT.Exp, scale=-1.0).then_inc(lf_act, 1)
            act.wait_ge(lf_dve, 3)
            A(lft[:, 3, :], lft[:, 2, :], ACT.Ln).then_inc(lf_act, 1)
            act.wait_ge(suffix_set, 2)
            act.dma_start(lfr.rearrange("g h t -> g (h t)"), lfc.rearrange("p a b -> p (a b)")).then_inc(suffix_out, 16)
            act.wait_ge(rope_set, 2 * NP + 1)
            act.wait_ge(lf_dve, 10)
            act.wait_ge(v_copied, 2 * TT)
            act.wait_ge(knew_set, 1)
            for m, (ko, vo) in enumerate((("k_a_p", "v_a_p"), ("win_k_p", "win_v_p"))):
                act.dma_start(O[ko], qkT[:, (2 * m + 1) * NP:(2 * m + 2) * NP, 0:SEQ]).then_inc(kv_out, 16)
                for t in range(QB):
                    act.dma_start(O[vo][t * P:t * P + P, :], v[:, t, m * W:m * W + W]).then_inc(kv_out, 16)
            act.dma_start(O["k_a_s"], qkT[:, NP:2 * NP, SEQ:T]).then_inc(kv_out, 16)
            act.dma_start(O["v_a_s"], v[0:NS, QB, 0:W]).then_inc(kv_out, 16)
            act.dma_start(O["win_k_s"][:, PAST - 1, :], knew).then_inc(kv_out, 16)
            act.dma_start(O["win_v_s"][:, PAST - 1, :], v[0:NS, QB, W:2 * W]).then_inc(kv_out, 16)
            act.dma_start(O["lf"], lfs[:, :]).then_inc(kv_out, 16)

            act.wait_ge(kv_out, 16 * 15)
            act.sem_inc(pB_copied, 1)
            act.sem_inc(p_copied, 1)
            act.wait_ge(cols_set, 1)
            with act.Fori(0, NS // 2) as i:
                for u in range(2):
                    if u == 0:
                        act.wait_ge(s_set, i * 16 + 2)
                        for n in range(4):
                            last = nc.scalar.copy(stage[:, n, :],
                                                  qkT[:, ds(i + n * NP, 1), 0:SEQ].rearrange("p a b -> p (a b)"))
                            last.then_inc(staged if n == 3 else lf_act, 1)
                    act.wait_ge(decay_ready, i * 2 + (u + 1))
                    nc.scalar.copy(decay, pb[6][:, :]).then_inc(decay_set, 1)
                    act.wait_ge(sA_max, i * 2 + (u + 1))
                    A(sA, sA, ACT.Exp, bias=dnm[:, 0:1], accum_out=dls[:, 0:1]).then_inc(pA_ready, 1)
                    act.wait_ge(sB_max, i * 2 + (u + 1))
                    A(sB, sB, ACT.Exp, bias=dnm[:, 1:2], accum_out=dls[:, 1:2]).then_inc(pB_ready, 1)

                    def copy_p(n):
                        q = n % QB
                        act.wait_ge(p_turned, i * 16 + (8 * u + n + 1))
                        nc.scalar.copy(pT[:, n % 2, 0:q + 1, :].rearrange("p a b -> p (a b)"), pb[6][:, 0:(q + 1) * P]
                                       ).then_inc(p_copied, 1)

                    for n in range(2 * QB):
                        m, q = n // QB, n % QB
                        nk = (q + 1) * P
                        act.wait_ge(s_set, i * 16 + (8 * u + n + 3))
                        A(sx[:, n % 2, 0:nk], sx[:, n % 2, 0:nk], ACT.Exp, bias=nm[:, m, q:q + 1],
                          accum_out=lsum[:, m, q:q + 1]).then_inc(p_ready, 1)
                        if n >= 1:
                            copy_p(n - 1)
                    copy_p(2 * QB - 1)
                    act.wait_ge(pA_turned, i * 2 + (u + 1))
                    nc.scalar.copy(pdA.rearrange("p a b -> p (a b)"), pb[5][:, 0:PAGES * H]).then_inc(lf_act, 1)
                    nc.scalar.copy(pdo[:, 0, :], pb[5][0:NS, PAGES * H:(PAGES + 1) * H]).then_inc(pA_copied, 1)
                    act.wait_ge(pB_turned, i * 2 + (u + 1))
                    nc.scalar.copy(pdB.rearrange("p a b -> p (a b)"), pb[2][:, 0:3 * H]).then_inc(lf_act, 1)
                    nc.scalar.copy(pdo[:, 1, :], pb[2][0:NS, 3 * H:4 * H]).then_inc(pB_copied, 1)
            scalar_after(act)


OUTS = {
    "y": (T, D), "k_a_p": (P, NP, SEQ), "v_a_p": (SEQ, W), "lf": (H, T), "win_k_p": (P, NP, SEQ), "win_v_p": (SEQ, W),
    "k_a_s": (P, NP, NS), "v_a_s": (NS, W), "win_k_s": (NS, PAST, W), "win_v_s": (NS, PAST, W),
}


def layout(a):
    c = np.ascontiguousarray
    steps = np.concatenate([np.arange(1, P + 1) * d for _, d in PATTERNS])
    seen = PAST - steps
    cache_k = a["cache_k_a"][0][:, ::-1].reshape(NPHYS, PAGE, NP, 2 * DH).transpose(0, 3, 2, 1)
    wk = a["cache_win_k"][0][:, seen].reshape(NS, WK, NP, 2 * DH).transpose(0, 3, 2, 1)
    wv = a["cache_win_v"][0][:, seen].reshape(NS, 3, P, W).transpose(0, 2, 1, 3)
    pages = a["page_table"][:, ::-1]
    cols = lambda g: g.reshape(KC, P).T
    both = lambda g: np.concatenate([g, g])
    return {
        "consts": constants(),
        "c_cols": c(np.concatenate([a["c_prompt"], a["c_sample"]]).T.reshape(KC, P, 9).transpose(1, 0, 2)),
        "gains": c(np.stack([cols(a["g_norm_mix"][0]), cols(a["g_norm_ffn"][0]),
                             cols(np.concatenate([a["g_oa"][0], a["g_ob"][0]]))], -1)),
        "g_qk": c(np.stack([both(a[k][0]) for k in ("g_qa", "g_ka", "g_qb", "g_kb")], -1)),
        "b_ada": c(a["b_ada"][0].reshape(6 * KC, P).T),
        "b_f": c(a["b_f"][0][:, None]),
        "e_bias": c(np.broadcast_to(a["e_bias"][0], (P, NE))),
        "x": c(np.concatenate([a["x_prompt"][0], a["x_sample"][:, 0]])),
        "w_ada": a["w_ada"][0], "w_in": a["w_in"][0],
        "cache_k": c(cache_k), "cache_v": c(a["cache_v_a"][0][:, ::-1].reshape(NPHYS, PAGE, W)),
        "cache_lf": c(a["cache_lf_a"][0][:, ::-1].transpose(0, 2, 1)),
        "pages": c(pages.reshape(1, -1).astype(np.int32)), "page_rows": c(pages.reshape(-1, 1).astype(np.uint32)),
        "win_k": a["cache_win_k"][0].reshape(NS, PAST, W), "win_v": a["cache_win_v"][0].reshape(NS, PAST, W),
        "win_k_seen": c(wk), "win_v_seen": c(wv),
        "w_o": a["w_o"][0], "w_router": c(a["w_router"][0].reshape(KC, P, NE).transpose(1, 0, 2)),
        "w_gate_up": c(np.concatenate([a["w_gate"][0], a["w_up"][0]], -1)), "w_down": a["w_down"][0],
        "ws_gate_up": c(np.concatenate([a["ws_gate"][0], a["ws_up"][0]], -1)), "ws_down": a["ws_down"][0],
    }


def kernel(**inputs):
    import concourse.bacc as bacc
    from concourse.bass_utils import run_bass_kernel_spmd

    nc = bacc.Bacc("TRN2", target_bir_lowering=False, num_devices=1)
    arrays = {f"in_{k}": np.ascontiguousarray(v)
              for k, v in layout({k: np.asarray(v) for k, v in inputs.items()}).items()}
    I = {k[3:]: nc.dram_tensor(k, v.shape, mybir.dt.from_np(v.dtype), kind="ExternalInput").ap() for k, v in arrays.items()}
    O = {k: nc.dram_tensor(f"out_{k}", shape, F32, kind="ExternalOutput").ap() for k, shape in OUTS.items()}
    program(nc, I, O)
    r = run_bass_kernel_spmd(nc, [arrays], core_ids=[0]).results[0]
    o = {k: r[f"out_{k}"] for k in OUTS}
    heads = lambda a, n: a.reshape(1, n, -1, H, DH)
    kt = lambda a, n: a.transpose(2, 1, 0).reshape(n, W)
    return (
        o["y"][None, :SEQ], o["y"][SEQ:, None],
        heads(kt(o["k_a_p"], SEQ), 1), heads(o["v_a_p"], 1), o["lf"][:, :SEQ].T.reshape(1, 1, SEQ, H),
        heads(kt(o["win_k_p"], SEQ), 1), heads(o["win_v_p"], 1),
        heads(kt(o["k_a_s"], NS), NS), heads(o["v_a_s"], NS), o["lf"][:, SEQ:].T.reshape(1, NS, 1, H),
        heads(o["win_k_s"], NS), heads(o["win_v_s"], NS),
    )
```
